# Optimizing a Trainium2 kernel written in Bass

```python
import math
import jax, jax.numpy as jnp
from jax import lax
import numpy as np

D_MODEL = 2048
BATCH = 1
SEQ = 256
DEPTH = 1

HEAD_DIM = 128
A_Q_HEADS = 8
A_KV_HEADS = 2
A_GROUP = A_Q_HEADS // A_KV_HEADS
A_HALF_WINDOW = 128
B_PATTERNS = ((128, 1), (512, 4), (2048, 16))
B_GROUPS = 3
B_HEADS_PER_GROUP = 4
B_HEADS = B_GROUPS * B_HEADS_PER_GROUP
B_HALF_SPAN = 64
N_BUCKETS = 32
MAX_DISTANCE = 1024
N_ATTN_HEADS = A_Q_HEADS + B_HEADS
PEER_HEADS = 8
PEER_NKEYS = 128
PEER_EXPERTS = PEER_NKEYS * PEER_NKEYS
PEER_QDIM = 256
PEER_TOPK = 16
PEER_TOKEN_BLOCK = 128
EPS = 1e-6
A_Q_W = A_Q_HEADS * HEAD_DIM
A_KV_W = A_KV_HEADS * HEAD_DIM
B_W = B_HEADS * HEAD_DIM
B_OUT_W = B_HEADS_PER_GROUP * HEAD_DIM
IN_WIDTH = A_Q_W + 2 * A_KV_W + 3 * B_W + 2 * D_MODEL

kernel_name = "hybrid_gated_swa_dilated_peer"

def rms_norm(x, g):
    xf = x.astype(jnp.float32)
    y = xf * lax.rsqrt(jnp.mean(xf * xf, axis=-1, keepdims=True) + EPS)
    return (y * g.astype(jnp.float32)).astype(x.dtype)

def t5_bucket(rel):
    half = N_BUCKETS // 2
    max_exact = half // 2
    ret = jnp.where(rel > 0, half, 0)
    n = jnp.abs(rel)
    nf = jnp.maximum(n, 1).astype(jnp.float32)
    large = max_exact + (jnp.log(nf / max_exact) / math.log(MAX_DISTANCE / max_exact) * (half - max_exact)).astype(jnp.int32)
    large = jnp.minimum(large, half - 1)
    return ret + jnp.where(n < max_exact, n, large)

def banded_attention(q, k, v, half_w, dist_scale, bias_table, sink, with_lse):
    dt = q.dtype
    n, hk, g, l, hd = q.shape
    blk = half_w
    nb = -(-l // blk)
    pad = nb * blk - l
    q = jnp.pad(q, ((0, 0), (0, 0), (0, 0), (0, pad), (0, 0)))
    kp = jnp.pad(k, ((0, 0), (0, 0), (blk, blk + pad), (0, 0))).reshape(n, hk, nb + 2, blk, hd)
    vp = jnp.pad(v, ((0, 0), (0, 0), (blk, blk + pad), (0, 0))).reshape(n, hk, nb + 2, blk, hd)
    kb = jnp.concatenate([kp[:, :, :-2], kp[:, :, 1:-1], kp[:, :, 2:]], axis=3)
    vb = jnp.concatenate([vp[:, :, :-2], vp[:, :, 1:-1], vp[:, :, 2:]], axis=3)
    qb = q.reshape(n, hk, g, nb, blk, hd)
    s = jnp.einsum('nhgbqd,nhbkd->nhgbqk', qb, kb, preferred_element_type=jnp.float32) * (hd ** -0.5)
    delta = jnp.arange(3 * blk)[None, :] - blk - jnp.arange(blk)[:, None]
    bias = bias_table[t5_bucket(delta * dist_scale)].astype(jnp.float32)
    bias = jnp.transpose(bias, (2, 3, 0, 1))[:, :, None]
    kpos = jnp.arange(nb)[:, None] * blk - blk + jnp.arange(3 * blk)[None, :]
    valid = (jnp.abs(delta) <= half_w)[None] & ((kpos >= 0) & (kpos < l))[:, None, :]
    s = jnp.where(valid, s + bias, -jnp.inf)
    m = jnp.max(s, axis=-1)
    if sink is not None:
        sk = sink.astype(jnp.float32)[None, :, :, None, None]
        m = jnp.maximum(m, sk)
    p = jnp.exp(s - m[..., None])
    denom = jnp.sum(p, axis=-1)
    if sink is not None:
        denom = denom + jnp.exp(sk - m)
    o = jnp.einsum('nhgbqk,nhbkd->nhgbqd', p, vb.astype(jnp.float32)) / denom[..., None]
    o = o.reshape(n, hk, g, nb * blk, hd)[:, :, :, :l].astype(dt)
    if with_lse:
        lse = (m + jnp.log(denom)).reshape(n, hk, g, nb * blk)[..., :l]
        return o, lse
    return o, None

def to_strided(t, d):
    b, s, h, hd = t.shape
    return t.reshape(b, s // d, d, h, hd).transpose(0, 2, 3, 1, 4).reshape(b * d, h, s // d, hd)

def from_strided(t, b, d):
    _, h, l, hd = t.shape
    return t.reshape(b, d, h, l, hd).transpose(0, 3, 1, 2, 4).reshape(b, l * d, h, hd)

def mixer_windowed_gqa(q, k, v, bias_a, sink):
    b, s, _ = q.shape
    qh = q.reshape(b, s, A_KV_HEADS, A_GROUP, HEAD_DIM).transpose(0, 2, 3, 1, 4)
    kh = k.reshape(b, s, A_KV_HEADS, HEAD_DIM).transpose(0, 2, 1, 3)
    vh = v.reshape(b, s, A_KV_HEADS, HEAD_DIM).transpose(0, 2, 1, 3)
    o, _ = banded_attention(qh, kh, vh, A_HALF_WINDOW, 1,
                            bias_a.reshape(N_BUCKETS, A_KV_HEADS, A_GROUP),
                            sink.reshape(A_KV_HEADS, A_GROUP), False)
    return o.transpose(0, 3, 1, 2, 4).reshape(b, s, A_Q_W)

def mixer_dilated(q, k, v, bias_b):
    b, s, _ = q.shape
    gw = B_HEADS_PER_GROUP * HEAD_DIM
    outs, lses = [], []
    for gi in range(B_GROUPS):
        d = B_PATTERNS[gi][1]
        sl = slice(gi * gw, (gi + 1) * gw)
        qg = to_strided(q[..., sl].reshape(b, s, B_HEADS_PER_GROUP, HEAD_DIM), d)[:, :, None]
        kg = to_strided(k[..., sl].reshape(b, s, B_HEADS_PER_GROUP, HEAD_DIM), d)
        vg = to_strided(v[..., sl].reshape(b, s, B_HEADS_PER_GROUP, HEAD_DIM), d)
        tb = bias_b[:, gi * B_HEADS_PER_GROUP:(gi + 1) * B_HEADS_PER_GROUP][:, :, None]
        o, lse = banded_attention(qg, kg, vg, B_HALF_SPAN, d, tb, None, True)
        outs.append(from_strided(o[:, :, 0], b, d).astype(jnp.float32))
        lses.append(lse[:, :, 0].reshape(b, d, B_HEADS_PER_GROUP, s // d).transpose(0, 3, 1, 2).reshape(b, s, B_HEADS_PER_GROUP))
    w = jax.nn.softmax(jnp.stack(lses, axis=0), axis=0)
    o = jnp.sum(w[..., None] * jnp.stack(outs, axis=0), axis=0)
    return o.reshape(b, s, B_OUT_W).astype(q.dtype)

def peer_ffn(h, w_pq, sub_keys, expert_u, expert_v):
    b, s, d = h.shape
    t = h.reshape(b * s, d)
    n_tok = b * s
    q = (t @ w_pq).reshape(n_tok, PEER_HEADS, 2, PEER_QDIM // 2)
    sc = jnp.einsum('thcd,hckd->thck', q, sub_keys, preferred_element_type=jnp.float32)
    top_s, top_i = lax.top_k(sc, PEER_TOPK)
    cand_s = (top_s[:, :, 0, :, None] + top_s[:, :, 1, None, :]).reshape(n_tok, PEER_HEADS, PEER_TOPK * PEER_TOPK)
    cand_i = (top_i[:, :, 0, :, None] * PEER_NKEYS + top_i[:, :, 1, None, :]).reshape(n_tok, PEER_HEADS, PEER_TOPK * PEER_TOPK)
    best_s, best_j = lax.top_k(cand_s, PEER_TOPK)
    expert_idx = jnp.take_along_axis(cand_i, best_j, axis=-1)
    gate = jax.nn.softmax(best_s, axis=-1)
    nblk = n_tok // PEER_TOKEN_BLOCK

    def block_fn(args):
        tb, ib, gb = args
        u = expert_u[ib]
        a = jax.nn.gelu(jnp.einsum('thkd,td->thk', u, tb, preferred_element_type=jnp.float32), approximate=False)
        vv = expert_v[ib]
        return jnp.einsum('thk,thkd->td', (gb * a).astype(vv.dtype), vv)

    out = lax.map(block_fn, (t.reshape(nblk, PEER_TOKEN_BLOCK, d),
                             expert_idx.reshape(nblk, PEER_TOKEN_BLOCK, PEER_HEADS, PEER_TOPK),
                             gate.reshape(nblk, PEER_TOKEN_BLOCK, PEER_HEADS, PEER_TOPK)))
    return out.reshape(b, s, d).astype(h.dtype)

def setup_inputs(seed: int = 0) -> dict:
    key = jax.random.key(seed)
    ks = jax.random.split(key, 16)
    f32 = jnp.float32
    nrm = lambda k, shape, scale: jax.random.normal(k, shape, f32) * scale
    return {
        "x": nrm(ks[0], (BATCH, SEQ, D_MODEL), 1.0),
        "rel_bias": nrm(ks[1], (N_BUCKETS, N_ATTN_HEADS), 0.5),
        "norm_mix_g": 1.0 + nrm(ks[2], (DEPTH, D_MODEL), 0.01),
        "w_in": nrm(ks[3], (DEPTH, D_MODEL, IN_WIDTH), D_MODEL ** -0.5),
        "sink_a": nrm(ks[4], (DEPTH, A_Q_HEADS), 0.5),
        "w_oa": nrm(ks[5], (DEPTH, A_Q_W, D_MODEL), A_Q_W ** -0.5),
        "w_ob": nrm(ks[6], (DEPTH, B_OUT_W, D_MODEL), B_OUT_W ** -0.5),
        "w_out": nrm(ks[7], (DEPTH, D_MODEL, D_MODEL), D_MODEL ** -0.5),
        "norm_ffn_g": 1.0 + nrm(ks[8], (DEPTH, D_MODEL), 0.01),
        "peer_wq": nrm(ks[9], (DEPTH, D_MODEL, PEER_HEADS * PEER_QDIM), D_MODEL ** -0.5),
        "peer_keys": nrm(ks[10], (DEPTH, PEER_HEADS, 2, PEER_NKEYS, PEER_QDIM // 2), (PEER_QDIM // 2) ** -0.5),
        "peer_u": nrm(ks[11], (DEPTH, PEER_EXPERTS, D_MODEL), D_MODEL ** -0.5),
        "peer_v": nrm(ks[12], (DEPTH, PEER_EXPERTS, D_MODEL), PEER_HEADS ** -0.5),
        "norm_final_g": 1.0 + nrm(ks[13], (D_MODEL,), 0.01),
    }

def reference(x, rel_bias, norm_mix_g, w_in, sink_a, w_oa, w_ob, w_out, norm_ffn_g,
              peer_wq, peer_keys, peer_u, peer_v, norm_final_g):
    splits = [A_Q_W, A_KV_W, A_KV_W, B_W, B_W, B_W, D_MODEL, D_MODEL]
    bounds = [int(c) for c in np.cumsum(splits)[:-1]]
    bias_a = rel_bias[:, :A_Q_HEADS]
    bias_b = rel_bias[:, A_Q_HEADS:]
    for layer in range(DEPTH):
        h = rms_norm(x, norm_mix_g[layer])
        proj = jnp.einsum('bsd,de->bse', h, w_in[layer])
        qa, ka, va, qb, kb, vb, ga, gb = jnp.split(proj, bounds, axis=-1)
        ya = mixer_windowed_gqa(qa, ka, va, bias_a, sink_a[layer]) @ w_oa[layer]
        yb = mixer_dilated(qb, kb, vb, bias_b) @ w_ob[layer]
        merged = jax.nn.sigmoid(ga) * ya + jax.nn.sigmoid(gb) * yb
        x = x + merged @ w_out[layer]
        h = rms_norm(x, norm_ffn_g[layer])
        x = x + peer_ffn(h, peer_wq[layer], peer_keys[layer], peer_u[layer], peer_v[layer])
    return rms_norm(x, norm_final_g)


_drawn_inputs = setup_inputs


def setup_inputs(seed=0):
    import zlib

    import numpy as np

    out = dict(_drawn_inputs(seed))
    spreads = {}
    factors = {'norm_mix_g': 6.396, 'sink_a': 8.0, 'norm_ffn_g': 22.984, 'norm_final_g': 30.776}
    for name, (base, spread) in spreads.items():
        noise = np.random.default_rng([zlib.crc32(name.encode()), seed]).standard_normal(out[name].shape)
        drawn = base * np.exp(spread * noise) if base else spread * noise
        out[name] = __import__('jax').numpy.asarray(drawn.astype(out[name].dtype))
    for name, factor in factors.items():
        out[name] = (out[name] * factor).astype(out[name].dtype)
    return out
```

```python
from contextlib import ExitStack

import numpy as np

import concourse.bass as bass
from concourse import mybir

F32 = mybir.dt.float32
F32R = mybir.dt.float32r
BF16 = mybir.dt.bfloat16
U32 = mybir.dt.uint32
ALU = mybir.AluOpType
ACT = mybir.ActivationFunctionType
AX = mybir.AxisListType

P = 128
T = 256
TT = T // P
D = 2048
KT = D // P
HD = 128
A_Q, A_KV = 8, 2
A_GROUP = A_Q // A_KV
B_G, B_S = 3, 4
B_H = B_G * B_S
HEADS = A_Q + B_H
B_PATTERNS = ((128, 1), (512, 4), (2048, 16))
N_BUCKETS, MAX_DISTANCE = 32, 1024
SCALE = HD ** -0.5
PH, NK, TOPK = 8, 128, 16
HC = 2 * PH
EPS = 1e-6
NEG = -1e30
LOWEST = -3.0e38

CW = 1024
RAW, LOS = 4, 2
BODY = 4

N_QK, N_V, N_GATE = A_Q + B_H + A_KV + B_H, A_KV + B_H, 2 * KT
CHUNKS = {"qk": 2 * N_QK, "v": 2 * N_V, "gate": 2 * N_GATE, "oa": KT, "ob": KT // 2,
          "out": 2 * KT, "pq": 2 * HC, "u": 2 * NK, "down": 2 * NK}
BLOCKS = {"qk": N_QK, "v": N_V, "gate": N_GATE, "oa": KT, "ob": KT, "out": KT, "pq": HC, "u": NK}
CHUNK0, BLOCK0 = {}, {}
_c = _b = 0
for _n in CHUNKS:
    CHUNK0[_n], BLOCK0[_n] = _c, _b
    _c += CHUNKS[_n]
    _b += BLOCKS.get(_n, 0)
N_CHUNKS = _c

N_BIAS = 384
N_DELTA = 512
N_ROWS = N_BUCKETS + 1 + B_G


def bias_rows():
    delta = np.arange(N_DELTA) - (T - 1)
    half = N_BUCKETS // 2
    exact = half // 2
    n = np.abs(delta)
    nf = np.maximum(n, 1).astype(np.float32)
    large = exact + (np.log(nf / np.float32(exact)) / np.float32(np.log(MAX_DISTANCE / exact))
                     * np.float32(half - exact)).astype(np.int32)
    bucket = np.where(delta > 0, half, 0) + np.where(n < exact, n, np.minimum(large, half - 1))
    rows = np.zeros((N_ROWS, N_DELTA), np.float32)
    rows[bucket, np.arange(N_DELTA)] = 1.0
    rows[N_BUCKETS] = np.where(n <= 128, 0.0, NEG)
    for g, (window, d) in enumerate(B_PATTERNS):
        inside = (delta % d == 0) & (n <= window // 2 // d * d)
        rows[N_BUCKETS + 1 + g] = np.where(inside, 0.0, NEG)
    return rows


def head_kinds():
    kinds = np.zeros((1 + B_G, HEADS), np.float32)
    kinds[0, :A_Q] = 1.0
    for g in range(B_G):
        kinds[1 + g, A_Q + g * B_S:A_Q + (g + 1) * B_S] = 1.0
    return kinds


class Steps:

    def __init__(self, eng, sem):
        self.eng, self.sem, self.base, self.n, self.it, self.per = eng, sem, 0, 0, None, 0

    def loop(self, it, per):
        self.it, self.per, self.n = it, per, 0

    def end_loop(self, count):
        assert self.n == self.per, (self.n, self.per)
        self.base += self.per * count
        self.it, self.n = None, 0

    def did(self, ins):
        ins.then_inc(self.sem, 1)
        self.n += 1
        return ins

    def wait(self):
        at = self.base + self.n
        self.eng.wait_ge(self.sem, at if self.it is None else self.it * self.per + at)

    def flat(self):
        self.base += self.n
        self.n = 0


def build(nc, A, out):
    with ExitStack() as ctx:
        def sem(name):
            return ctx.enter_context(nc.semaphore(name))

        total = nc.sbuf_bytes_remaining // 32 * 32 - 32
        ctx.enter_context(nc.sbuf_tensor("slab", [P, total], mybir.dt.uint8))
        base = nc.sbuf_base - total
        KB = 1024
        RING, MOVE = base, base + 40 * KB
        ARENA = MOVE + 32 * KB
        MISC = ARENA + 128 * KB
        end = base + total

        def at(name, off, shape, dt=F32):
            return nc.alloc_sbuf_tensor_at(name, shape, dt, offset=off)

        raw = [at(f"raw{i}", RING + i * 4 * KB, [P, CW]) for i in range(RAW)]
        hi = [at(f"hi{i}", RING + (4 + i) * 4 * KB, [P, CW], F32R) for i in range(RAW)]
        lo = [at(f"lo{i}", RING + (8 + i) * 4 * KB, [P, CW], F32R) for i in range(LOS)]
        move = at("move", MOVE, [P, KT, 2 * T], F32R)

        misc = [MISC]

        def small(name, shape, dt=F32):
            n = int(np.prod(shape[1:])) * 4
            t = at(name, misc[0], shape, dt)
            misc[0] += -(-n // 32) * 32
            assert misc[0] <= end, name
            return t

        upper = [small(f"upper{i}", [P, T]) for i in range(2)]
        ident = small("ident", [P, P])
        ones = small("ones", [P, P])
        flip = small("flip", [P, P])
        g_mix = small("g_mix", [P, KT])
        g_ffn = small("g_ffn", [P, KT])
        sinks = small("sinks", [P, A_Q])
        neg_sinks = small("neg_sinks", [P, A_Q])
        stat = small("stat", [P, 8])
        expert_i = small("expert_i", [P, T])
        expert_j = small("expert_j", [P, T])
        gate_t = small("gate_t", [P, T])

        qk = at("qk", ARENA, [P, N_QK, T])
        v_nat = at("v_nat", ARENA + 34 * KB, [P, TT, N_V, HD])
        gates = at("gates", ARENA + 48 * KB, [P, 2 * KT, T])
        bias = at("bias", ARENA + 80 * KB, [P, HEADS, N_BIAS])
        prob = at("prob", ARENA + 110 * KB, [P, 2, B_G, T])
        prob_t = at("prob_t", ARENA + 116 * KB, [P, B_G, TT, T])
        q_now = at("q_now", ARENA + 122 * KB, [P, B_G, T])
        v_now = at("v_now", ARENA + 125 * KB, [P, TT, B_G, HD])
        v_t = [at(f"v_t{i}", ARENA + (116 + i) * KB, [P, T]) for i in range(2)]
        x_t = at("x_t", ARENA + 48 * KB, [P, KT, T])
        x_sq = at("x_sq", ARENA + 64 * KB, [P, KT, T])
        rows_sb = at("rows_sb", ARENA + 116 * KB, [N_ROWS, N_DELTA])
        table_sb = at("table_sb", ARENA + 118 * KB, [N_ROWS, HEADS])
        line_sb = at("line_sb", ARENA + 110 * KB, [HEADS, N_DELTA])
        ssq = at("ssq", ARENA + 122 * KB, [P, T])
        mean = at("mean", ARENA + 123 * KB, [P, T])
        rstd = at("rstd", ARENA + 124 * KB, [P, T])
        work = at("work", ARENA + 125 * KB, [P, T])
        hankel = at("hankel", ARENA, [P, HEADS, N_BIAS])
        att = at("att", ARENA + 80 * KB, [P, A_Q + B_S, 2 * T], F32R)
        sig = [at(f"sig{i}", ARENA + (104 + i) * KB, [P, T]) for i in range(2)]
        merged = [at(f"merged{i}", ARENA + (106 + i) * KB, [P, T]) for i in range(2)]
        x_again = at("x_again", ARENA, [P, KT, T])
        x1 = at("x1", ARENA + 16 * KB, [P, KT, T])
        sq1 = [at(f"sq1{i}", ARENA + (108 + i) * KB, [P, T]) for i in range(2)]
        h2 = at("h2", ARENA + 48 * KB, [P, KT, T])
        x1_nat = at("x1_nat", ARENA + 64 * KB, [P, TT, D])
        keys_sb = at("keys_sb", ARENA + 80 * KB, [P, HC, NK])
        query = [at(f"query{i}", ARENA + (88 + i) * KB, [P, T]) for i in range(2)]
        score = [at(f"score{i}", ARENA + (90 + i) * KB, [P, TT, NK]) for i in range(2)]
        score_b = at("score_b", ARENA + 92 * KB, [P, TT, NK])
        top_now = [at(f"top_now{i}", ARENA + 94 * KB + i * 128, [P, TT, TOPK]) for i in range(2)]
        idx_now = [at(f"idx_now{i}", ARENA + 94 * KB + 256 + i * 128, [P, TT, TOPK], U32) for i in range(2)]
        top_s = at("top_s", ARENA + 100 * KB, [P, TT, PH, 2, TOPK])
        top_i = at("top_i", ARENA + 102 * KB, [P, TT, PH, 2, TOPK])
        cand = at("cand", ARENA + 104 * KB, [P, TOPK * TOPK])
        cand_b = at("cand_b", ARENA + 105 * KB, [P, TOPK * TOPK])
        pick = at("pick", ARENA + 106 * KB, [P, TOPK, TOPK])
        pick_b = at("pick_b", ARENA + 107 * KB, [P, TOPK, TOPK])
        best_s = at("best_s", ARENA + 108 * KB, [P, TOPK])
        best_j = at("best_j", ARENA + 108 * KB + 64, [P, TOPK], U32)
        half_u = at("half_u", ARENA + 108 * KB + 128, [P, 2, TOPK], U32)
        half_f = at("half_f", ARENA + 108 * KB + 256, [P, 2, TOPK])
        soft = at("soft", ARENA + 108 * KB + 384, [P, TOPK])
        soft_s = at("soft_s", ARENA + 108 * KB + 448, [P, 4])
        iota16 = at("iota16", ARENA + 113 * KB, [P, TOPK])
        found_i = at("found_i", ARENA + 109 * KB, [P, TT, PH * TOPK])
        found_j = at("found_j", ARENA + 110 * KB, [P, TT, PH * TOPK])
        found_g = at("found_g", ARENA + 111 * KB, [P, TT, PH * TOPK])
        act = at("act", ARENA, [P, NK, T])
        iota128 = at("iota128", MOVE, [P, P])
        one_i = [at(f"one_i{i}", MOVE + KB + i * 2 * KB, [P, 4, P]) for i in range(2)]
        one_j = [at(f"one_j{i}", MOVE + 5 * KB + i * 2 * KB, [P, 4, P]) for i in range(2)]
        act_hi = [at(f"act_hi{i}", MOVE + 10 * KB + i * KB, [P, T], F32R) for i in range(2)]
        act_lo = [at(f"act_lo{i}", MOVE + 12 * KB + i * KB, [P, T], F32R) for i in range(2)]
        x2 = at("x2", MOVE + 14 * KB, [P, TT, D])
        zero = at("zero", MOVE + 30 * KB, [P, 512], BF16)
        g_final = at("g_final", ARENA, [P, D])
        squares = at("squares", ARENA + 8 * KB, [P, D])
        y = at("y", ARENA + 16 * KB, [P, TT, D])

        ps = [ctx.enter_context(nc.psum_tensor(f"ps{i}", [P, 512], F32)) for i in range(8)]

        line_dram = nc.dram_tensor("line_scratch", [HEADS * N_DELTA], F32)
        x1_dram = nc.dram_tensor("x1_scratch", [P, TT * D], F32)

        small_in, x_in, keys_in, x_again_in, bias_in = sem("small_in"), sem("x_in"), sem("keys_in"), sem("x_again_in"), sem("bias_in")
        raw_landed = [sem(f"raw_landed{i}") for i in range(RAW)]
        hi_ready = sem("hi_ready")
        lo_ready = sem("lo_ready")
        chunk_used = sem("chunk_used")
        upper_ready = sem("upper_ready")
        block_summed = sem("block_summed")
        dve_step, act_step = sem("dve_step"), sem("act_step")
        consts = sem("consts")
        settled = sem("settled")
        line_sum, line_ready, line_out = sem("line_sum"), sem("line_ready"), sem("line_out")
        bias_flipped, bias_ready = sem("bias_flipped"), sem("bias_ready")
        sq_ready, ssq_ready, ssq_sum = sem("sq_ready"), sem("ssq_ready"), sem("ssq_sum")
        inv_ready, root_ready = sem("inv_ready"), sem("root_ready")
        norm_ready, norm_hi, move_ready = sem("norm_ready"), sem("norm_hi"), sem("move_ready")
        vt_turned, vn_ready = sem("vt_turned"), sem("vn_ready")
        q_staged, v_staged = sem("q_staged"), sem("v_staged")
        scores_done, max_ready, exp_done, prob_ready = (
            sem("scores_done"), sem("max_ready"), sem("exp_done"), sem("prob_ready"))
        prob_turned, prob_copied, pv_done, o_ready = (
            sem("prob_turned"), sem("prob_copied"), sem("pv_done"), sem("o_ready"))
        att_hi, att_ready = sem("att_hi"), sem("att_ready")
        sig_ready, merged_ready, merged_hi, merged_lo = (
            sem("sig_ready"), sem("merged_ready"), sem("merged_hi"), sem("merged_lo"))
        x1_ready, x1_sq, sq_added = sem("x1_ready"), sem("x1_sq"), sem("sq_added")
        x1_turned, x1_copied, x1_out = sem("x1_turned"), sem("x1_copied"), sem("x1_out")
        key_scores, score_ready, top_ready, top_kept = (
            sem("key_scores"), sem("score_ready"), sem("top_ready"), sem("top_kept"))
        best_ready, soft_ready, found_ready = sem("best_ready"), sem("soft_ready"), sem("found_ready")
        iota_ready, found_turned, experts_ready = sem("iota_ready"), sem("found_turned"), sem("experts_ready")
        act_ready, move_free = sem("act_ready"), sem("move_free")
        one_i_ready, one_j_ready, gates_spread, gated = (
            sem("one_i_ready"), sem("one_j_ready"), sem("gates_spread"), sem("gated"))
        act_hi_ready, act_lo_ready = sem("act_hi_ready"), sem("act_lo_ready")
        zero_ready, down_done = sem("zero_ready"), sem("down_done")
        x2_in, g_final_in, x2_ready, x2_sq, y_ready, y_out = (
            sem("x2_in"), sem("g_final_in"), sem("x2_ready"), sem("x2_sq"), sem("y_ready"), sem("y_out"))

        block = ctx.enter_context(nc.Block())

        def flat(ap):
            return ap.rearrange("p a t -> p (a t)")

        def pick1(t, i):
            return flat(t[:, bass.ds(i, 1), :])

        @block.sync
        def _(sp):
            def load(name, it, s, first=False):
                c = CHUNK0[name] + BODY * it + s
                if not first:
                    sp.wait_ge(lo_ready, c - RAW + 1)
                src = A["w_" + name][bass.ds(BODY * it + s, 1), :, :].rearrange("a p n -> p (a n)")
                sp.dma_start(raw[s][:], src).then_inc(raw_landed[s], 16)

            sp.dma_start(x_t[:], A["x_t"]).then_inc(x_in, 16)
            for s in range(BODY):
                load("qk", 0, s, first=True)
            sp.dma_start(g_mix[:], A["g_mix"]).then_inc(small_in, 16)
            sp.dma_start(g_ffn[:], A["g_ffn"]).then_inc(small_in, 16)
            sp.dma_start(ident[:], A["ident"]).then_inc(small_in, 16)
            sp.dma_start(flip[:], A["flip"]).then_inc(small_in, 16)
            sp.dma_start(rows_sb[:], A["bias_rows"]).then_inc(small_in, 16)
            sp.dma_start(table_sb[0:N_BUCKETS, :], A["rel_bias"]).then_inc(small_in, 16)
            sp.dma_start(table_sb[N_BUCKETS:N_ROWS, :], A["head_kinds"]).then_inc(small_in, 16)
            sp.dma_start(sinks[:], spread(A["sink_a"], A_Q)).then_inc(small_in, 16)
            sp.wait_ge(line_ready, 1)
            sp.dma_start(line_dram.ap().rearrange("(h m) -> h m", h=HEADS), line_sb[:]).then_inc(line_out, 16)
            sp.wait_ge(line_out, 16)
            sp.dma_start(hankel[:], slant(line_dram)).then_inc(bias_in, 16)
            with sp.Fori(1, CHUNKS["qk"] // BODY) as it:
                for s in range(BODY):
                    load("qk", it, s)
            for name in ("v", "gate", "oa", "ob"):
                with sp.Fori(0, CHUNKS[name] // BODY) as it:
                    for s in range(BODY):
                        load(name, it, s)
                if name == "oa":
                    sp.wait_ge(att_ready, 1)
                    sp.dma_start(x_again[:], A["x_t"]).then_inc(x_again_in, 16)
            with sp.Fori(0, CHUNKS["out"] // BODY) as it:
                for s in range(BODY):
                    load("out", it, s)
            for s in range(BODY):
                load("pq", 0, s)
            sp.wait_ge(merged_lo, KT + 2)
            sp.dma_start(keys_sb[:], A["keys"]).then_inc(keys_in, 16)
            sp.wait_ge(x1_copied, 8)
            sp.dma_start(x1_dram.ap(), x1_nat[:].rearrange("p a d -> p (a d)")).then_inc(x1_out, 16)
            with sp.Fori(1, CHUNKS["pq"] // BODY) as it:
                for s in range(BODY):
                    load("pq", it, s)
            with sp.Fori(0, CHUNKS["u"] // BODY) as it:
                for s in range(BODY):
                    load("u", it, s)
            for s in range(BODY):
                load("down", 0, s)
            sp.wait_ge(x1_out, 16)
            sp.wait_ge(move_free, 1)
            sp.dma_start(x2[:].rearrange("p a d -> p (a d)"), x1_dram.ap()).then_inc(x2_in, 16)
            with sp.Fori(1, CHUNKS["down"] // BODY // 2) as it:
                for s in range(BODY):
                    load("down", it, s)
            sp.wait_ge(act_lo_ready, 40)
            sp.dma_start(g_final[:], spread(A["g_final"], D)).then_inc(g_final_in, 16)
            with sp.Fori(CHUNKS["down"] // BODY // 2, CHUNKS["down"] // BODY) as it:
                for s in range(BODY):
                    load("down", it, s)
            for tt in range(TT):
                sp.wait_ge(y_ready, tt + 1)
                sp.dma_start(out[tt * P:(tt + 1) * P, :], y[:, tt, :]).then_inc(y_out, 16)
            sp.wait_ge(y_out, 16 * TT)

        @block.gpsimd
        def _(pool):
            pool.wait_ge(block_summed, BLOCK0["v"] + 2)
            with pool.Fori(0, A_Q) as h:
                pool.wait_ge(scores_done, h + 1)
                nc.gpsimd.tensor_copy(q_now[:, 0, :], pick1(qk, h)).then_inc(q_staged, 1)
            with pool.Fori(0, B_S) as s:
                pool.wait_ge(scores_done, s + A_Q + 1)
                heads = qk[:, A_Q:A_Q + B_H, :].rearrange("p (g s) t -> p g s t", s=B_S)
                nc.gpsimd.tensor_copy(q_now[:], heads[:, :, bass.ds(s, 1), :].rearrange("p g a t -> p g (a t)")
                                      ).then_inc(q_staged, 1)
                pool.wait_ge(vn_ready, N_V + 2)
                pool.wait_ge(pv_done, s + A_Q)
                for tt in range(TT):
                    vs = v_nat[:, tt, A_KV:, :].rearrange("p (g s) d -> p g s d", s=B_S)
                    nc.gpsimd.tensor_copy(v_now[:, tt, :, :], vs[:, :, bass.ds(s, 1), :].rearrange("p g a d -> p g (a d)")
                                          ).then_inc(v_staged, 1)
            pool.wait_ge(att_ready, 1)
            nc.gpsimd.iota(iota16[:], [[1, TOPK]], base=0, channel_multiplier=0,
                           allow_small_or_imprecise_dtypes=True).then_inc(iota_ready, 1)
            pool.wait_ge(move_free, 1)
            nc.gpsimd.iota(iota128[:], [[1, P]], base=0, channel_multiplier=0,
                           allow_small_or_imprecise_dtypes=True).then_inc(iota_ready, 1)
            nc.gpsimd.memset(zero[:], 0.0).then_inc(zero_ready, 1)

        @block.scalar
        def _(a):
            def hi_of(cb, it, s):
                slot = s % RAW
                a.wait_ge(raw_landed[slot], it * 16 + (cb // 4 + s // 4) * 16 + 16)
                a.wait_ge(chunk_used, it * BODY + cb + s + 1)
                nc.scalar.copy(hi[slot][:], raw[slot][:]).then_inc(hi_ready, 1)

            def upper_of(b, bank, used):
                a.wait_ge(chunk_used, used + RAW)
                a.wait_ge(block_summed, b + 1)
                nc.scalar.copy(upper[bank][:], ps[bank][:, T:2 * T]).then_inc(upper_ready, 1)

            def body(name, it, after=None):
                c0, b0 = CHUNK0[name], BLOCK0[name]
                for s in range(BODY):
                    hi_of(c0, it, s + 2)
                    if name == "oa":
                        upper_of(it * 4 + b0 + s, s % 2, it * BODY + c0 + s + 1)
                    elif name == "ob":
                        for e in range(2):
                            upper_of(it * 8 + b0 + 2 * s + e, e, it * BODY + c0 + s + 1)
                            if after:
                                after(it, 2 * s + e)
                        continue
                    elif s % 2:
                        upper_of(it * 2 + b0 + s // 2, s // 2, it * BODY + c0 + s + 1)
                    if after:
                        after(it, s)

            for ring in (vn_ready, score_ready, top_kept):
                a.sem_inc(ring, 2)
            a.sem_inc(o_ready, 1)

            a.wait_ge(x_in, 16)
            nc.scalar.activation(x_sq[:], x_t[:], ACT.Square).then_inc(sq_ready, 1)
            hi_of(0, 0, 0)
            hi_of(0, 0, 1)
            a.wait_ge(line_sum, 1)
            nc.scalar.copy(line_sb[:], ps[6][0:HEADS, :]).then_inc(line_ready, 1)
            a.wait_ge(inv_ready, 1)
            nc.scalar.activation(rstd[:], work[:], ACT.Sqrt).then_inc(root_ready, 1)
            for q in range(4):
                a.wait_ge(norm_ready, 4 * q + 4)
                nc.scalar.copy(move[:, 4 * q:4 * q + 4, 0:T], x_sq[:, 4 * q:4 * q + 4, :]).then_inc(norm_hi, 1)
            for h in range(HEADS):
                a.wait_ge(bias_flipped, h + 1)
                nc.scalar.copy(bias[:, h, :], ps[6 + h % 2][:, 0:N_BIAS]).then_inc(bias_ready, 1)
            with a.Fori(0, CHUNKS["qk"] // BODY) as it:
                body("qk", it)

            def keep_v(it, s):
                if s == 3:
                    for e in range(2):
                        n = it * 2 + e
                        a.wait_ge(vt_turned, n + 3)
                        nc.scalar.copy(v_nat[:, :, bass.ds(n, 1), :].rearrange("p t a d -> p t (a d)"),
                                       ps[6 + e][:, 0:T].rearrange("p (t d) -> p t d", t=TT)).then_inc(vn_ready, 1)
            with a.Fori(0, CHUNKS["v"] // BODY) as it:
                body("v", it, keep_v)

            def heads_a(h, s):
                if s == 0:
                    a.wait_ge(max_ready, h + 1)
                    for u in range(2):
                        nc.scalar.activation(prob[:, u, 0, :], prob[:, u, 0, :], ACT.Exp, bias=stat[:, u:u + 1],
                                             accum_out=stat[:, 2 + u:3 + u]).then_inc(exp_done, 1)
                    nc.scalar.activation(stat[:, 4:6], stat[:, 0:2], ACT.Exp, bias=sinks[:, bass.ds(h, 1)]
                                         ).then_inc(exp_done, 1)
                if s == 2:
                    a.wait_ge(prob_turned, h + 2)
                    nc.scalar.copy(prob_t[:, 0, :, :], ps[3][:].rearrange("p (k q) -> p k q", k=TT)).then_inc(prob_copied, 1)
                if s == 3:
                    a.wait_ge(pv_done, h + 1)
                    nc.scalar.copy(pick1(qk, h), ps[5][:, 0:T]).then_inc(o_ready, 1)
            with a.Fori(0, A_Q) as h:
                body("gate", h, heads_a)

            with a.Fori(0, B_S) as s4:
                def heads_b(half):
                    def f(it, s):
                        if half == 0 and s == 3:
                            a.wait_ge(max_ready, s4 + A_Q + 1)
                            for u in range(2):
                                nc.scalar.activation(prob[:, u, :, :], prob[:, u, :, :], ACT.Exp, bias=stat[:, u:u + 1],
                                                     accum_out=stat[:, 2 + u:3 + u]).then_inc(exp_done, 1)
                        if half == 1 and s == 2:
                            a.wait_ge(prob_turned, s4 + A_Q + 2)
                            for g in range(B_G):
                                nc.scalar.copy(prob_t[:, g, :, :], ps[2 + g][:].rearrange("p (k q) -> p k q", k=TT)
                                               ).then_inc(prob_copied, 1)
                        if half == 1 and s == 3:
                            a.wait_ge(pv_done, s4 + A_Q + 1)
                            nc.scalar.copy(pick1(qk, s4 + A_Q), ps[5][:, 0:T]).then_inc(o_ready, 1)
                    return f
                body("gate", s4 * 2 + A_Q, heads_b(0))
                body("gate", s4 * 2 + A_Q + 1, heads_b(1))
            a.wait_ge(o_ready, A_Q + B_S + 1)
            nc.scalar.copy(att[:, :, 0:T], qk[:, 0:A_Q + B_S, :]).then_inc(att_hi, 1)

            def gate_a(it, s):
                n = it * 4 + s
                a.wait_ge(merged_ready, n + 1)
                nc.scalar.activation(sig[s % 2][:], pick1(gates, n), ACT.Sigmoid).then_inc(sig_ready, 1)
            with a.Fori(0, CHUNKS["oa"] // BODY) as it:
                body("oa", it, gate_a)

            def gate_b(it, s):
                n = it * 8 + s
                a.wait_ge(merged_ready, n + KT + 1)
                nc.scalar.activation(sig[s % 2][:], pick1(gates, n + KT), ACT.Sigmoid).then_inc(sig_ready, 1)
                a.wait_ge(merged_ready, n + KT + 3)
                nc.scalar.copy(move[:, bass.ds(n, 1), 0:T].rearrange("p a t -> p (a t)"), merged[s % 2][:]
                               ).then_inc(merged_hi, 1)
            with a.Fori(0, CHUNKS["ob"] // BODY) as it:
                body("ob", it, gate_b)

            def square(it, s):
                if s % 2:
                    n = it * 2 + s // 2
                    a.wait_ge(x1_ready, n + 1)
                    a.wait_ge(sq_added, n + 1)
                    nc.scalar.activation(sq1[s // 2][:], pick1(x1, n), ACT.Square).then_inc(x1_sq, 1)
            with a.Fori(0, CHUNKS["out"] // BODY) as it:
                body("out", it, square)
            for n in range(8):
                a.wait_ge(x1_turned, n + 1)
                nc.scalar.copy(x1_nat[:, n // 4, (n % 4) * 512:(n % 4) * 512 + 512], ps[6 + n % 2][:]).then_inc(x1_copied, 1)
            a.wait_ge(inv_ready, 2)
            nc.scalar.activation(rstd[:], work[:], ACT.Sqrt).then_inc(root_ready, 1)
            for q in range(4):
                a.wait_ge(norm_ready, KT + 4 * q + 4)
                nc.scalar.copy(move[:, 4 * q:4 * q + 4, 0:T], h2[:, 4 * q:4 * q + 4, :]).then_inc(norm_hi, 1)

            def keep_scores(it, s):
                if s == 3:
                    for e in range(2):
                        n = it * 2 + e
                        a.wait_ge(key_scores, n + 3)
                        a.wait_ge(top_ready, n + 1)
                        nc.scalar.copy(score[e][:], ps[6 + e][:, 0:T].rearrange("p (t k) -> p t k", t=TT)).then_inc(score_ready, 1)
                    for e in range(2):
                        n = it * 2 + e
                        a.wait_ge(top_ready, n + 3)
                        nc.scalar.copy(top_s[:].rearrange("p t h c k -> p t (h c) k")[:, :, bass.ds(n, 1), :]
                                       .rearrange("p t a k -> p t (a k)"), top_now[e][:])
                        nc.scalar.copy(top_i[:].rearrange("p t h c k -> p t (h c) k")[:, :, bass.ds(n, 1), :]
                                       .rearrange("p t a k -> p t (a k)"), idx_now[e][:]).then_inc(top_kept, 1)
            with a.Fori(0, CHUNKS["pq"] // BODY) as it:
                body("pq", it, keep_scores)

            def gelu(it, s):
                if s % 2:
                    j = it * 2 + s // 2
                    a.wait_ge(block_summed, j + BLOCK0["u"] + 3)
                    nc.scalar.activation(pick1(act, j), upper[s // 2][:], ACT.Gelu).then_inc(act_ready, 1)

            def gelu_and_softmax(it, s):
                if s == 2:
                    a.wait_ge(best_ready, it + 1)
                    nc.scalar.activation(soft[:], best_s[:], ACT.Exp, bias=soft_s[:, 0:1], accum_out=soft_s[:, 1:2]
                                         ).then_inc(soft_ready, 1)
                gelu(it, s)
            UR = TT * PH
            a.wait_ge(x1_out, 16)
            with a.Fori(0, UR) as it:
                body("u", it, gelu_and_softmax)
            for n, t in enumerate((expert_i, expert_j, gate_t)):
                a.wait_ge(found_turned, n + 1)
                nc.scalar.copy(t[:], ps[5 + n][:, 0:T]).then_inc(experts_ready, 1)
            with a.Fori(UR, CHUNKS["u"] // BODY) as it:
                body("u", it, gelu)

            def act_hi_of(j, r):
                a.wait_ge(chunk_used, j * 2 + CHUNK0["down"] - 2 + RAW)
                nc.scalar.copy(act_hi[r][:], pick1(act, j)).then_inc(act_hi_ready, 1)

            a.wait_ge(gated, T // 4 + 2)
            act_hi_of(0, 0)

            def down(it, last=False):
                c0 = CHUNK0["down"]
                for s in range(BODY):
                    if not (last and s >= 2):
                        hi_of(c0, it, s + 2)
                    if s % 2 == 0 and not (last and s == 2):
                        act_hi_of(it * 2 + s // 2 + 1, (s // 2 + 1) % 2)
            with a.Fori(0, CHUNKS["down"] // BODY - 1) as it:
                down(it)
            down(CHUNKS["down"] // BODY - 1, last=True)
            a.wait_ge(down_done, 1)
            for tt in range(TT):
                a.wait_ge(x2_ready, 4 * tt + 4)
                if tt:
                    a.wait_ge(x2_sq, tt)
                nc.scalar.activation(squares[:], x2[:, tt, :], ACT.Square, accum_out=stat[:, tt:tt + 1]).then_inc(x2_sq, 1)
            a.wait_ge(inv_ready, 3)
            nc.scalar.activation(stat[:, 4:6], stat[:, 2:4], ACT.Sqrt).then_inc(root_ready, 1)

        @block.vector
        def _(v):
            me = Steps(v, dve_step)
            did, wait = me.did, me.wait

            def lo_of(cb, it, s):
                v.wait_ge(hi_ready, it * BODY + cb + s + 1)
                v.wait_ge(chunk_used, it * BODY + cb + s - LOS + 1 + RAW)
                nc.vector.tensor_tensor(lo[s % LOS][:], raw[s % RAW][:], hi[s % RAW][:].bitcast(F32), ALU.subtract
                                        ).then_inc(lo_ready, 1)

            def sum_of(b, bank, dst):
                v.wait_ge(upper_ready, b + 1)
                nc.vector.tensor_tensor(dst, ps[bank][:, 0:T], upper[bank][:], ALU.add).then_inc(block_summed, 1)

            def rsqrt_of(m, w, r, n):
                nc.vector.reciprocal(w, m).then_inc(inv_ready, 1)
                v.wait_ge(root_ready, n)
                for o, x0, x1_ in ((w, r, r), (w, w, m)):
                    did(nc.vector.tensor_tensor(o, x0, x1_, ALU.mult))
                    wait()
                did(nc.vector.tensor_scalar(w, w, -0.5, 1.5, ALU.mult, ALU.add))
                wait()
                did(nc.vector.tensor_tensor(r, r, w, ALU.mult))
                wait()

            def normed(src, dst, g, n0):
                for k in range(KT):
                    nc.vector.scalar_tensor_tensor(out=dst[:, k, :], in0=src[:, k, :], scalar=g[:, k:k + 1],
                                                   in1=rstd[:], op0=ALU.mult, op1=ALU.mult).then_inc(norm_ready, 1)
                for q in range(4):
                    v.wait_ge(norm_hi, 4 * n0 + q + 1)
                    nc.vector.tensor_tensor(move[:, 4 * q:4 * q + 4, T:2 * T], dst[:, 4 * q:4 * q + 4, :],
                                            move[:, 4 * q:4 * q + 4, 0:T].bitcast(F32), ALU.subtract).then_inc(move_ready, 1)

            def settle():
                v.sem_inc(settled, 1)

            def body(name, it, after=None):
                for s in range(BODY):
                    lo_of(CHUNK0[name], it, s + 1)
                    if after:
                        after(it, s)

            v.sem_inc(block_summed, 2)
            v.sem_inc(top_ready, 2)
            v.sem_inc(merged_ready, 2)
            v.sem_inc(merged_lo, 2)
            v.sem_inc(sq_added, 2)
            v.sem_inc(gated, 2)

            nc.vector.memset(ones[:], 1.0).then_inc(consts, 1)
            v.wait_ge(sq_ready, 1)
            nc.vector.tensor_reduce(ssq[:], x_sq[:].rearrange("p k t -> p t k"), AX.X, ALU.add).then_inc(ssq_ready, 1)
            v.wait_ge(ssq_sum, 1)
            did(nc.vector.tensor_scalar(mean[:], ps[5][:, 0:T], 1.0 / D, EPS, ALU.mult, ALU.add))
            wait()
            rsqrt_of(mean[:], work[:], rstd[:], 1)
            v.wait_ge(small_in, 16 * 8)
            normed(x_t, x_sq, g_mix, 0)
            did(nc.vector.tensor_scalar(neg_sinks[:], sinks[:], -1.0, None, ALU.mult))
            lo_of(0, 0, 0)
            me.flat()

            def keep_qk(it, s):
                if s % 2:
                    n = it * 2 + s // 2
                    sum_of(n + BLOCK0["qk"], s // 2, pick1(qk, n))
            with v.Fori(0, CHUNKS["qk"] // BODY) as it:
                body("qk", it, keep_qk)

            def keep_vt(it, s):
                if s % 2:
                    n = it * 2 + s // 2
                    v.wait_ge(vt_turned, n + 1)
                    sum_of(n + BLOCK0["v"], s // 2, v_t[s // 2][:])
            with v.Fori(0, CHUNKS["v"] // BODY) as it:
                body("v", it, keep_vt)

            def biased(h, g, u, bank, off):
                did(nc.vector.scalar_tensor_tensor(
                    out=prob[:, u, g, :], in0=ps[bank][:, u * T:(u + 1) * T], scalar=SCALE,
                    in1=flat(bias[:, bass.ds(h, 1), off:off + T]), op0=ALU.mult, op1=ALU.add))

            def keep_gate(it, s):
                if s % 2:
                    n = it * 2 + s // 2
                    sum_of(n + BLOCK0["gate"], s // 2, pick1(gates, n))

            def divided(n, w):
                did(nc.vector.reciprocal(stat[:, 6:8], stat[:, 2:4]))
                wait()
                for u in range(2):
                    nc.vector.tensor_scalar(prob[:, u, 0:w, :], prob[:, u, 0:w, :], stat[:, 6 + u:7 + u], None, ALU.mult
                                            ).then_inc(prob_ready, 1)

            v.wait_ge(bias_ready, HEADS)
            with v.Fori(0, A_Q) as h:
                me.loop(h, 5)

                def heads_a(it, s):
                    if s == 0:
                        v.wait_ge(scores_done, h + 2)
                        v.wait_ge(prob_turned, h + 1)
                        for u in range(2):
                            biased(h, 0, u, 2, P - u * P)
                        wait()
                        did(nc.vector.tensor_reduce(stat[:, 0:2], prob[:, :, 0, :], AX.X, ALU.max, negate=True))
                        wait()
                        nc.vector.tensor_scalar(stat[:, 0:2], stat[:, 0:2], neg_sinks[:, bass.ds(h, 1)], None, ALU.min
                                                ).then_inc(max_ready, 1)
                    if s == 1:
                        v.wait_ge(exp_done, h * 3 + 3)
                        did(nc.vector.tensor_tensor(stat[:, 2:4], stat[:, 2:4], stat[:, 4:6], ALU.add))
                        wait()
                        divided(h, 1)
                    keep_gate(it, s)
                body("gate", h, heads_a)
            me.end_loop(A_Q)

            with v.Fori(0, B_S) as s4:
                me.loop(s4, 7)

                def heads_b(half):
                    def f(it, s):
                        if half == 0 and s < 3:
                            if s == 0:
                                v.wait_ge(scores_done, s4 + A_Q + 2)
                                v.wait_ge(prob_turned, s4 + A_Q + 1)
                            for u in range(2):
                                biased(s4 + (A_Q + s * B_S), s, u, 2 + s, P - u * P)
                        if half == 0 and s == 2:
                            wait()
                            nc.vector.tensor_reduce(stat[:, 0:2], prob[:], AX.XY, ALU.max, negate=True).then_inc(max_ready, 1)
                        if half == 1 and s == 0:
                            v.wait_ge(exp_done, s4 * 2 + 3 * A_Q + 2)
                            divided(s4, B_G)
                        keep_gate(it, s)
                    return f
                body("gate", s4 * 2 + A_Q, heads_b(0))
                body("gate", s4 * 2 + A_Q + 1, heads_b(1))
            me.end_loop(B_S)
            v.wait_ge(att_hi, 1)
            nc.vector.tensor_tensor(att[:, :, T:2 * T], qk[:, 0:A_Q + B_S, :], att[:, :, 0:T].bitcast(F32), ALU.subtract
                                    ).then_inc(att_ready, 1)

            with v.Fori(0, CHUNKS["oa"] // BODY) as it:
                def gate_a(it, s):
                    n = it * 4 + s
                    e = s % 2
                    sum_of(n + BLOCK0["oa"], e, merged[e][:])
                    v.wait_ge(block_summed, n + BLOCK0["oa"] + 3)
                    v.wait_ge(sig_ready, n + 1)
                    nc.vector.tensor_tensor(pick1(gates, n), merged[e][:], sig[e][:], ALU.mult).then_inc(merged_ready, 1)
                body("oa", it, gate_a)
            with v.Fori(0, CHUNKS["ob"] // BODY) as it:
                me.loop(it, 2 * BODY)

                def gate_b(it, s):
                    for e in range(2):
                        n = it * 8 + (2 * s + e)
                        v.wait_ge(merged_lo, n + 1)
                        sum_of(n + BLOCK0["ob"], e, merged[e][:])
                        v.wait_ge(block_summed, n + BLOCK0["ob"] + 3)
                        v.wait_ge(sig_ready, n + KT + 1)
                        did(nc.vector.tensor_tensor(merged[e][:], merged[e][:], sig[e][:], ALU.mult))
                        wait()
                        nc.vector.tensor_tensor(merged[e][:], merged[e][:], pick1(gates, n), ALU.add).then_inc(merged_ready, 1)
                    for e in range(2):
                        n = it * 8 + (2 * s + e)
                        v.wait_ge(merged_hi, n + 1)
                        nc.vector.tensor_tensor(move[:, bass.ds(n, 1), T:2 * T].rearrange("p a t -> p (a t)"), merged[e][:],
                                                move[:, bass.ds(n, 1), 0:T].rearrange("p a t -> p (a t)").bitcast(F32),
                                                ALU.subtract).then_inc(merged_lo, 1)
                body("ob", it, gate_b)
            me.end_loop(CHUNKS["ob"] // BODY)

            nc.vector.memset(ssq[:], 0.0).then_inc(ssq_ready, 1)
            v.wait_ge(ssq_ready, 2)
            v.wait_ge(x_again_in, 16)
            with v.Fori(0, CHUNKS["out"] // BODY) as it:
                def keep_x1(it, s):
                    if s % 2:
                        n = it * 2 + s // 2
                        sum_of(n + BLOCK0["out"], s // 2, pick1(x1, n))
                        v.wait_ge(block_summed, n + BLOCK0["out"] + 3)
                        nc.vector.tensor_tensor(pick1(x1, n), pick1(x1, n), pick1(x_again, n), ALU.add).then_inc(x1_ready, 1)
                        v.wait_ge(x1_sq, n + 1)
                        v.wait_ge(sq_added, n + 2)
                        nc.vector.tensor_tensor(ssq[:], ssq[:], sq1[s // 2][:], ALU.add).then_inc(sq_added, 1)
                body("out", it, keep_x1)
            v.wait_ge(ssq_sum, 2)
            did(nc.vector.tensor_scalar(mean[:], ps[5][:, 0:T], 1.0 / D, EPS, ALU.mult, ALU.add))
            wait()
            rsqrt_of(mean[:], work[:], rstd[:], 2)
            normed(x1, h2, g_ffn, 1)
            me.flat()

            with v.Fori(0, CHUNKS["pq"] // BODY) as it:
                me.loop(it, 16)

                def rank(it, s):
                    if s % 2:
                        n = it * 2 + s // 2
                        v.wait_ge(key_scores, n + 1)
                        sum_of(n + BLOCK0["pq"], s // 2, query[s // 2][:])
                    if s == 3:
                        for e in range(2):
                            n = it * 2 + e
                            v.wait_ge(score_ready, n + 3)
                            v.wait_ge(top_kept, n + 1)
                            top, idx, sc = top_now[e], idx_now[e], score[e]
                            settle()
                            for tt in range(TT):
                                did(nc.vector.max(top[:, tt, 0:8], sc[:, tt, :]))
                            wait()
                            settle()
                            for tt in range(TT):
                                did(nc.vector.match_replace(score_b[:, tt, :], top[:, tt, 0:8], sc[:, tt, :], LOWEST))
                            for tt in range(TT):
                                did(nc.vector.max_index(idx[:, tt, 0:8], top[:, tt, 0:8], sc[:, tt, :]))
                            wait()
                            settle()
                            for tt in range(TT):
                                did(nc.vector.max(top[:, tt, 8:16], score_b[:, tt, :]))
                            wait()
                            settle()
                            nc.vector.max_index(idx[:, 0, 8:16], top[:, 0, 8:16], score_b[:, 0, :])
                            nc.vector.max_index(idx[:, 1, 8:16], top[:, 1, 8:16], score_b[:, 1, :]).then_inc(top_ready, 1)
                body("pq", it, rank)
            me.end_loop(CHUNKS["pq"] // BODY)

            def keep_u(it, s):
                if s % 2:
                    j = it * 2 + s // 2
                    sum_of(j + BLOCK0["u"], s // 2, upper[s // 2][:])

            v.wait_ge(iota_ready, 1)
            v.wait_ge(top_kept, HC + 2)
            with v.Fori(0, TT * PH) as it:
                me.loop(it, 16)
                halves = top_s[:].rearrange("p t h c k -> p (t h) c k")
                rows = top_i[:].rearrange("p t h c k -> p (t h) c k")

                def best(it, s):
                    if s == 0:
                        a = halves[:, bass.ds(it, 1), 0, :].rearrange("p a k -> p (a k)").unsqueeze(2).to_broadcast([P, TOPK, TOPK])
                        b = halves[:, bass.ds(it, 1), 1, :].rearrange("p a k -> p (a k)").unsqueeze(1).to_broadcast([P, TOPK, TOPK])
                        did(nc.vector.tensor_tensor(cand[:].rearrange("p (a b) -> p a b", a=TOPK), a, b, ALU.add))
                        wait()
                        settle()
                        did(nc.vector.max(best_s[:, 0:8], cand[:]))
                        wait()
                        settle()
                        did(nc.vector.match_replace(cand_b[:], best_s[:, 0:8], cand[:], LOWEST))
                    if s == 1:
                        did(nc.vector.max_index(best_j[:, 0:8], best_s[:, 0:8], cand[:]))
                        did(nc.vector.tensor_scalar(soft_s[:, 0:1], best_s[:, 0:1], -1.0, None, ALU.mult))
                        wait()
                        settle()
                        nc.vector.max(best_s[:, 8:16], cand_b[:]).then_inc(best_ready, 1)
                        v.wait_ge(best_ready, it + 1)
                    if s == 2:
                        did(nc.vector.max_index(best_j[:, 8:16], best_s[:, 8:16], cand_b[:]))
                        wait()
                        did(nc.vector.tensor_scalar(half_u[:, 0, :], best_j[:], 4, None, ALU.logical_shift_right))
                        did(nc.vector.tensor_scalar(half_u[:, 1, :], best_j[:], 15, None, ALU.bitwise_and))
                        wait()
                        did(nc.vector.tensor_copy(half_f[:], half_u[:]))
                        wait()
                        did(one(0))
                        wait()
                        did(own(it, 0))
                    if s == 3:
                        wait()
                        did(put(it, 0, found_i))
                        wait()
                        did(one(1))
                        wait()
                        did(own(it, 1))
                        wait()
                        did(put(it, 1, found_j))
                        v.wait_ge(soft_ready, it + 1)
                        did(nc.vector.reciprocal(soft_s[:, 2:3], soft_s[:, 1:2]))
                        wait()
                        nc.vector.tensor_scalar(pick_found(found_g, it), soft[:], soft_s[:, 2:3], None, ALU.mult
                                                ).then_inc(found_ready, 1)
                    keep_u(it, s)

                def pick_found(t, it):
                    return t[:].rearrange("p t (h k) -> p (t h) k", k=TOPK)[:, bass.ds(it, 1), :].rearrange("p a k -> p (a k)")

                def one(c):
                    return nc.vector.tensor_tensor(pick[:], half_f[:, c, :].unsqueeze(2).to_broadcast([P, TOPK, TOPK]),
                                                   iota16[:].unsqueeze(1).to_broadcast([P, TOPK, TOPK]), ALU.is_equal)

                def own(it, c):
                    r = rows[:, bass.ds(it, 1), c, :].rearrange("p a k -> p (a k)").unsqueeze(1).to_broadcast([P, TOPK, TOPK])
                    return nc.vector.tensor_tensor(pick_b[:], pick[:], r, ALU.mult)

                def put(it, c, dst):
                    return nc.vector.tensor_reduce(pick_found(dst, it), pick_b[:], AX.X, ALU.add)
                body("u", it, best)
            me.end_loop(TT * PH)
            with v.Fori(TT * PH, CHUNKS["u"] // BODY) as it:
                body("u", it, keep_u)

            v.wait_ge(experts_ready, 3)
            v.wait_ge(iota_ready, 2)
            v.wait_ge(act_ready, NK)

            def gated_of(it, r):
                v.wait_ge(gates_spread, 2 * it + (r + 3))
                a4 = act[:, :, bass.ds(8 * it + 4 * r, 4)].rearrange("p j u -> p u j")
                nc.vector.tensor_tensor(a4, a4, ps[r][:].rearrange("p (u j) -> p u j", u=4), ALU.mult).then_inc(gated, 1)

            def ones_of(it, r):
                v.wait_ge(gates_spread, 2 * it + (r + 1))
                for u in range(4):
                    t = 8 * it + (4 * r + u)
                    nc.vector.tensor_scalar(one_i[r][:, u, :], iota128[:], expert_i[:, bass.ds(t, 1)], None,
                                            ALU.is_equal).then_inc(one_i_ready, 1)
                    nc.vector.tensor_scalar(one_j[r][:, u, :], iota128[:], expert_j[:, bass.ds(t, 1)],
                                            gate_t[:, bass.ds(t, 1)], ALU.is_equal, ALU.mult).then_inc(one_j_ready, 1)
            for r in range(2):
                ones_of(0, r)
            with v.Fori(0, T // 8 - 1) as it:
                for r in range(2):
                    gated_of(it, r)
                    ones_of(it + 1, r)
            for r in range(2):
                gated_of(T // 8 - 1, r)

            def act_lo_of(j, r):
                v.wait_ge(act_hi_ready, j + 1)
                nc.vector.tensor_tensor(act_lo[r][:], pick1(act, j), act_hi[r][:].bitcast(F32), ALU.subtract
                                        ).then_inc(act_lo_ready, 1)
            v.wait_ge(gated, T // 4 + 2)
            act_lo_of(0, 0)

            def down(it, last=False):
                for s in range(BODY):
                    if not (last and s == 3):
                        lo_of(CHUNK0["down"], it, s + 1)
                    if s % 2 == 0 and not (last and s == 2):
                        act_lo_of(it * 2 + (s // 2 + 1), (s // 2 + 1) % 2)
            with v.Fori(0, CHUNKS["down"] // BODY - 1) as it:
                down(it)
            down(CHUNKS["down"] // BODY - 1, last=True)

            v.wait_ge(down_done, 1)
            v.wait_ge(x2_in, 16)
            for tt in range(TT):
                for c in range(4):
                    x = x2[:, tt, c * 512:(c + 1) * 512]
                    nc.vector.tensor_tensor(x, ps[4 * tt + c][:], x, ALU.add).then_inc(x2_ready, 1)
            v.wait_ge(x2_sq, 2)
            did(nc.vector.tensor_scalar(stat[:, 0:2], stat[:, 0:2], 1.0 / D, EPS, ALU.mult, ALU.add))
            wait()
            rsqrt_of(stat[:, 0:2], stat[:, 2:4], stat[:, 4:6], 3)
            v.wait_ge(g_final_in, 16)
            for tt in range(TT):
                nc.vector.scalar_tensor_tensor(out=y[:, tt, :], in0=x2[:, tt, :], scalar=stat[:, 4 + tt:5 + tt],
                                               in1=g_final[:], op0=ALU.mult, op1=ALU.mult).then_inc(y_ready, 1)

        @block.tensor
        def _(pe):
            def products(slot, lslot, items):
                for n, (bank, col, m, first, last) in enumerate(items):
                    def high():
                        return nc.tensor.matmul(ps[bank][:], hi[slot][:, col:col + P], m, start=first, stop=last)

                    def low():
                        return nc.tensor.matmul(ps[bank][:, 0:T], lo[lslot][:, col:col + P], m[:, 0:T], start=False,
                                                stop=False, skip_group_check=True)
                    if last:
                        low()
                        ins = high()
                    else:
                        high()
                        ins = low()
                ins.then_inc(chunk_used, 1)

            def body(name, it, src=move, after=None):
                c0, b0 = CHUNK0[name], BLOCK0[name]
                for s in range(BODY):
                    if name == "oa":
                        b = it * 4 + (b0 + s)
                        items = [(s % 2, k * P, src[:, k, :], k == 0, k == 7) for k in range(8)]
                    elif name == "ob":
                        b = it * 8 + (b0 + 2 * s)
                        items = [(e, (4 * e + k) * P, src[:, A_Q + k, :], k == 0, k == 3) for e in range(2) for k in range(4)]
                    else:
                        b = it * 2 + (b0 + s // 2)
                        half = s % 2
                        items = [(s // 2, k * P, src[:, 8 * half + k, :], half == 0 and k == 0, half == 1 and k == 7)
                                 for k in range(8)]
                    pe.wait_ge(lo_ready, it * BODY + (c0 + s + 1))
                    if name in ("oa", "ob") or s % 2 == 0:
                        pe.wait_ge(block_summed, b + (2 if name == "ob" else 1))
                    products(s % RAW, s % LOS, items)
                    if after:
                        after(it, s)

            pe.sem_inc(chunk_used, RAW)
            pe.sem_inc(vt_turned, 2)
            pe.sem_inc(scores_done, 1)
            pe.sem_inc(prob_turned, 1)
            pe.sem_inc(key_scores, 2)
            pe.sem_inc(gates_spread, 2)

            pe.wait_ge(consts, 1)
            pe.wait_ge(ssq_ready, 1)
            nc.tensor.matmul(ps[5][:, 0:T], ones[:], ssq[:], start=True, stop=True).then_inc(ssq_sum, 1)
            pe.wait_ge(small_in, 16 * 8)
            nc.tensor.matmul(ps[6][0:HEADS, :], table_sb[:], rows_sb[:], start=True, stop=True).then_inc(line_sum, 1)

            pe.wait_ge(bias_in, 16)
            pe.wait_ge(line_ready, 1)
            for h in range(HEADS):
                if h >= 2:
                    pe.wait_ge(bias_ready, h - 1)
                nc.tensor.matmul(ps[6 + h % 2][:, 0:N_BIAS], flip[:], hankel[:, h, :], start=True, stop=True
                                 ).then_inc(bias_flipped, 1)
            pe.wait_ge(move_ready, 4)
            with pe.Fori(0, CHUNKS["qk"] // BODY) as it:
                body("qk", it)

            def turn_v(it, s):
                for e in ((0,) if s == 2 else (1,) if s == 3 else ()):
                    n = it * 2 + e
                    pe.wait_ge(block_summed, n + (BLOCK0["v"] + 3))
                    pe.wait_ge(vn_ready, n + 1)
                    for tt in range(TT):
                        ins = nc.tensor.transpose(ps[6 + e][:, tt * P:(tt + 1) * P], v_t[e][:, tt * P:(tt + 1) * P], ident[:])
                    ins.then_inc(vt_turned, 1)
            pe.wait_ge(line_ready, 1)
            with pe.Fori(0, CHUNKS["v"] // BODY) as it:
                body("v", it, after=turn_v)

            def scores(n, q, k, banks):
                pe.wait_ge(q_staged, n + 1)
                for g in range(q):
                    for u in range(2):
                        ins = nc.tensor.matmul(ps[banks + g][:, u * T:(u + 1) * T], q_now[:, g, u * P:(u + 1) * P], k(g),
                                               start=True, stop=True)
                ins.then_inc(scores_done, 1)

            def turn_p(n, groups, bank):
                pe.wait_ge(prob_ready, n * 2 + 2)
                for g in range(groups):
                    for k in range(TT):
                        for u in range(2):
                            ins = nc.tensor.transpose(ps[bank + g][:, k * T + u * P:k * T + (u + 1) * P],
                                                      prob[:, u, g, k * P:(k + 1) * P], ident[:])
                ins.then_inc(prob_turned, 1)

            def times_v(n, copied, groups, val):
                pe.wait_ge(prob_copied, copied)
                pe.wait_ge(o_ready, n + 1)
                for g in range(groups):
                    for k in range(TT):
                        ins = nc.tensor.matmul(ps[5][:, 0:T], val(g, k), prob_t[:, g, k, :], start=g == 0 and k == 0,
                                               stop=g == groups - 1 and k == TT - 1)
                ins.then_inc(pv_done, 1)

            pe.wait_ge(vn_ready, N_V + 2)
            for kv in range(A_KV):
                with pe.Fori(kv * A_GROUP, (kv + 1) * A_GROUP) as h:
                    def heads_a(it, s):
                        if s == 1:
                            turn_p(h, 1, 3)
                    scores(h, 1, lambda g: qk[:, A_Q + B_H + kv, :], 2)
                    body("gate", h, after=heads_a)
                    times_v(h, h + 1, 1, lambda g, k: v_nat[:, k, kv, :])
            with pe.Fori(0, B_S) as s4:
                def heads_b(it, s):
                    if s == 1:
                        turn_p(s4 + A_Q, B_G, 2)
                scores(s4 + A_Q, B_G, lambda g: pick1(qk, s4 + (A_Q + B_H + A_KV + g * B_S)), 2)
                body("gate", s4 * 2 + A_Q)
                body("gate", s4 * 2 + (A_Q + 1), after=heads_b)
                pe.wait_ge(v_staged, s4 * 2 + 2)
                times_v(s4 + A_Q, s4 * B_G + (A_Q + B_G), B_G, lambda g, k: v_now[:, k, g, :])

            pe.wait_ge(att_ready, 1)
            with pe.Fori(0, CHUNKS["oa"] // BODY) as it:
                body("oa", it, att)
            with pe.Fori(0, CHUNKS["ob"] // BODY) as it:
                body("ob", it, att)
            pe.wait_ge(merged_lo, KT + 2)
            with pe.Fori(0, CHUNKS["out"] // BODY) as it:
                body("out", it)

            pe.wait_ge(sq_added, KT + 2)
            nc.tensor.matmul(ps[5][:, 0:T], ones[:], ssq[:], start=True, stop=True).then_inc(ssq_sum, 1)
            for n in range(8):
                if n >= 2:
                    pe.wait_ge(x1_copied, n - 1)
                for k in range(4):
                    ins = nc.tensor.transpose(ps[6 + n % 2][:, k * P:(k + 1) * P],
                                              x1[:, n % 4 * 4 + k, n // 4 * P:(n // 4 + 1) * P], ident[:])
                ins.then_inc(x1_turned, 1)

            pe.wait_ge(move_ready, 8)
            pe.wait_ge(keys_in, 16)
            pe.wait_ge(x1_copied, 8)

            def score_keys(it, s):
                for e in ((0,) if s == 2 else (1,) if s == 3 else ()):
                    n = it * 2 + e
                    pe.wait_ge(block_summed, n + (BLOCK0["pq"] + 3))
                    pe.wait_ge(score_ready, n + 1)
                    for tt in range(TT):
                        ins = nc.tensor.matmul(ps[6 + e][:, tt * NK:(tt + 1) * NK], query[e][:, tt * P:(tt + 1) * P],
                                               pick1(keys_sb, n), start=True, stop=True)
                    ins.then_inc(key_scores, 1)
            with pe.Fori(0, CHUNKS["pq"] // BODY) as it:
                body("pq", it, after=score_keys)

            with pe.Fori(0, TT * PH) as it:
                body("u", it)
            pe.wait_ge(found_ready, TT * PH)
            for n, t in enumerate((found_i, found_j, found_g)):
                for tt in range(TT):
                    ins = nc.tensor.transpose(ps[5 + n][:, tt * P:(tt + 1) * P], t[:, tt, :], ident[:])
                ins.then_inc(found_turned, 1)
            with pe.Fori(TT * PH, CHUNKS["u"] // BODY) as it:
                body("u", it)
            pe.drain().then_inc(move_free, 1)

            pe.wait_ge(block_summed, BLOCK0["u"] + BLOCKS["u"] + 2)
            with pe.Fori(0, T // 8) as it:
                for r in range(2):
                    pe.wait_ge(one_i_ready, 8 * it + (4 * r + 4))
                    pe.wait_ge(one_j_ready, 8 * it + (4 * r + 4))
                    pe.wait_ge(gated, 2 * it + (r + 1))
                    for u in range(4):
                        ins = nc.tensor.matmul(ps[r][:, u * P:(u + 1) * P], one_i[r][:, u, :], one_j[r][:, u, :],
                                               start=True, stop=True)
                    ins.then_inc(gates_spread, 1)

            pe.wait_ge(zero_ready, 1)
            pe.wait_ge(gated, T // 4 + 2)
            pe.wait_ge(experts_ready, 3)
            for b in range(8):
                nc.tensor.matmul(ps[b][:], zero[:, 0:P], zero[:], start=True, stop=False)

            with pe.Fori(0, CHUNKS["down"] // BODY) as it:
                for s in range(BODY):
                    r = s // 2
                    pe.wait_ge(lo_ready, it * BODY + (CHUNK0["down"] + s + 1))
                    if s % 2 == 0:
                        pe.wait_ge(act_lo_ready, it * 2 + (r + 1))
                    for tt in range(TT):
                        for a, w in ((act_hi[r], hi[s]), (act_hi[r], lo[s % LOS]), (act_lo[r], hi[s])):
                            for c in range(2):
                                ins = nc.tensor.matmul(ps[4 * tt + 2 * (s % 2) + c][:], a[:, tt * P:(tt + 1) * P],
                                                       w[:, c * 512:(c + 1) * 512], start=False, stop=False,
                                                       skip_group_check=True)
                    ins.then_inc(chunk_used, 1)
            for b in range(8):
                ins = nc.tensor.matmul(ps[b][:], zero[:, 0:P], zero[:], start=False, stop=True)
            ins.then_inc(down_done, 1)


def spread(ap, n):
    return bass.AP(ap.tensor, 0, [[0, P], [1, n]])


def slant(line):
    return bass.AP(line, 0, [[1, P], [N_DELTA, HEADS], [1, N_BIAS]])


def columns(w, order=None):
    k, n = w.shape
    b = w.reshape(k // P, P, n // P, P).transpose(2, 1, 0, 3)
    if order is not None:
        b = b[order]
    b = b.reshape(b.shape[0], P, k)
    if k > CW:
        b = b.reshape(b.shape[0], P, k // CW, CW).transpose(0, 2, 1, 3)
    elif k < CW:
        b = b.reshape(b.shape[0] * k // CW, CW // k, P, k).transpose(0, 2, 1, 3)
    return np.ascontiguousarray(b.reshape(-1, P, CW))


def kernel(**inputs):
    import concourse.bacc as bacc
    from concourse.bass_utils import run_bass_kernel_spmd

    f = {k: np.asarray(v) for k, v in inputs.items()}
    aq, akv, b = A_Q, A_KV, B_H
    w_in = f["w_in"][0]
    order = np.arange(w_in.shape[1] // P)
    qa, ka, va, qb, kb, vb, rest = np.split(order, np.cumsum([aq, akv, akv, b, b, b]))
    x_t = np.ascontiguousarray(f["x"][0].reshape(T, KT, P).transpose(2, 1, 0))
    arrays = {
        "x_t": x_t,
        "g_mix": np.ascontiguousarray(f["norm_mix_g"][0].reshape(KT, P).T),
        "g_ffn": np.ascontiguousarray(f["norm_ffn_g"][0].reshape(KT, P).T),
        "g_final": f["norm_final_g"],
        "ident": np.eye(P, dtype=np.float32),
        "flip": np.ascontiguousarray(np.eye(P, dtype=np.float32)[::-1]),
        "bias_rows": bias_rows(),
        "head_kinds": head_kinds(),
        "rel_bias": f["rel_bias"],
        "sink_a": f["sink_a"][0],
        "keys": np.ascontiguousarray(f["peer_keys"][0].reshape(HC, NK, HD).transpose(2, 0, 1)),
        "w_qk": columns(w_in, np.concatenate([qa, qb, ka, kb])),
        "w_v": columns(w_in, np.concatenate([va, vb])),
        "w_gate": columns(w_in, rest),
        "w_oa": columns(f["w_oa"][0]),
        "w_ob": columns(f["w_ob"][0]),
        "w_out": columns(f["w_out"][0]),
        "w_pq": columns(f["peer_wq"][0]),
        "w_u": np.ascontiguousarray(f["peer_u"][0].reshape(NK, NK, 2, 8, P).transpose(1, 2, 4, 3, 0).reshape(-1, P, CW)),
        "w_down": np.ascontiguousarray(f["peer_v"][0].reshape(NK, NK, 2, CW).transpose(1, 2, 0, 3).reshape(-1, P, CW)),
    }
    nc = bacc.Bacc("TRN2", target_bir_lowering=False, num_devices=1)
    aps = {k: nc.dram_tensor(k, a.shape, F32, kind="ExternalInput").ap() for k, a in arrays.items()}
    out = nc.dram_tensor("out", [T, D], F32, kind="ExternalOutput").ap()
    build(nc, aps, out)
    r = run_bass_kernel_spmd(nc, [arrays], core_ids=[0])
    return r.results[0]["out"].reshape(1, T, D)
```

```python
from contextlib import ExitStack

import numpy as np

import concourse.bass as bass
from concourse import mybir

F32 = mybir.dt.float32
F32R = mybir.dt.float32r
BF16 = mybir.dt.bfloat16
U32 = mybir.dt.uint32
ALU = mybir.AluOpType
ACT = mybir.ActivationFunctionType
AX = mybir.AxisListType

P = 128
T = 256
TT = T // P
D = 2048
KT = D // P
HD = 128
A_Q, A_KV = 8, 2
A_GROUP = A_Q // A_KV
B_G, B_S = 3, 4
B_H = B_G * B_S
HEADS = A_Q + B_H
B_PATTERNS = ((128, 1), (512, 4), (2048, 16))
N_BUCKETS, MAX_DISTANCE = 32, 1024
SCALE = HD ** -0.5
PH, NK, TOPK = 8, 128, 16
HC = 2 * PH
EPS = 1e-6
NEG = -1e30
LOWEST = -3.0e38

CW = 1024
RAW, LOS = 4, 2
BODY = 4

N_QK, N_V, N_GATE = A_Q + B_H + A_KV + B_H, A_KV + B_H, 2 * KT
CHUNKS = {"qk": 2 * N_QK, "v": 2 * N_V, "gate": 2 * N_GATE, "oa": KT, "ob": KT // 2,
          "out": 2 * KT, "pq": 2 * HC, "u": 2 * NK, "down": 2 * NK}
BLOCKS = {"qk": N_QK, "v": N_V, "gate": N_GATE, "oa": KT, "ob": KT, "out": KT, "pq": HC, "u": NK}
CHUNK0, BLOCK0 = {}, {}
_c = _b = 0
for _n in CHUNKS:
    CHUNK0[_n], BLOCK0[_n] = _c, _b
    _c += CHUNKS[_n]
    _b += BLOCKS.get(_n, 0)

N_BIAS = 384
N_DELTA = 512
SLANT = 4
FLIP0 = CHUNKS["qk"] // BODY - HEADS // 2
N_ROWS = N_BUCKETS + 1 + B_G


def bias_rows():
    delta = np.arange(N_DELTA) - (T - 1)
    half = N_BUCKETS // 2
    exact = half // 2
    n = np.abs(delta)
    nf = np.maximum(n, 1).astype(np.float32)
    large = exact + (np.log(nf / np.float32(exact)) / np.float32(np.log(MAX_DISTANCE / exact))
                     * np.float32(half - exact)).astype(np.int32)
    bucket = np.where(delta > 0, half, 0) + np.where(n < exact, n, np.minimum(large, half - 1))
    rows = np.zeros((N_ROWS, N_DELTA), np.float32)
    rows[bucket, np.arange(N_DELTA)] = 1.0
    rows[N_BUCKETS] = np.where(n <= 128, 0.0, NEG)
    for g, (window, d) in enumerate(B_PATTERNS):
        inside = (delta % d == 0) & (n <= window // 2 // d * d)
        rows[N_BUCKETS + 1 + g] = np.where(inside, 0.0, NEG)
    return rows


def head_kinds():
    kinds = np.zeros((1 + B_G, HEADS), np.float32)
    kinds[0, :A_Q] = 1.0
    for g in range(B_G):
        kinds[1 + g, A_Q + g * B_S:A_Q + (g + 1) * B_S] = 1.0
    return kinds


UR = TT * PH + 1
U0 = UR + 2
J_KEPT = 2 * U0 - 1
PAIRS = T // 2
UG = U0 + PAIRS // BODY

TURN_BANKS = (2, 3, 4, 6, 7)
TURNS = len(TURN_BANKS)

ATT_PARTS = ((0, 4), (4, 8), (8, A_Q + B_S - 1), (A_Q + B_S - 1, A_Q + B_S))


class Steps:

    def __init__(self, eng, sem):
        self.eng, self.sem, self.base, self.n, self.it, self.per, self.first = eng, sem, 0, 0, None, 0, 0

    def loop(self, it, per, first=0):
        self.it, self.per, self.first, self.n = it, per, first, 0

    def end_loop(self, count):
        assert self.n == self.per, (self.n, self.per)
        self.base += self.per * count
        self.it, self.n = None, 0

    def did(self, ins):
        ins.then_inc(self.sem, 1)
        self.n += 1
        return ins

    def wait(self):
        at = self.base + self.n
        self.eng.wait_ge(self.sem, at if self.it is None else self.it * self.per + (at - self.first * self.per))

    def flat(self):
        self.base += self.n
        self.n = 0


def run(eng, body, name, *fs, steps=None, per=0, carried=(), carry=False):
    count = CHUNKS[name] // BODY

    def late(it, s):
        for f, lag in fs:
            if s >= lag or not (isinstance(it, int) and it == 0):
                f(it, s - lag)

    def first(it, s):
        carried_out(carried, s)
        late(it, s)
    body(name, 0, first)
    if steps:
        steps.flat()
    with eng.Fori(1, count) as it:
        if steps:
            steps.loop(it, per, 1)
        body(name, it, late)
    if steps:
        steps.end_loop(count - 1)
    left = [(f, lag, count) for f, lag in fs]
    if carry:
        return left
    for s in range(BODY):
        carried_out(left, s)
    if steps:
        steps.flat()


def carried_out(left, s):
    for f, lag, count in left:
        if s < lag:
            f(count, s - lag)


def build(nc, A, out):
    with ExitStack() as ctx:
        def sem(name):
            return ctx.enter_context(nc.semaphore(name))

        total = nc.sbuf_bytes_remaining // 32 * 32 - 32
        ctx.enter_context(nc.sbuf_tensor("slab", [P, total], mybir.dt.uint8))
        base = nc.sbuf_base - total
        KB = 1024
        RING, MOVE = base, base + 40 * KB
        ARENA = MOVE + 32 * KB
        MISC = ARENA + 128 * KB
        end = base + total

        def at(name, off, shape, dt=F32):
            return nc.alloc_sbuf_tensor_at(name, shape, dt, offset=off)

        raw = [at(f"raw{i}", RING + i * 4 * KB, [P, CW]) for i in range(RAW)]
        hi = [at(f"hi{i}", RING + (4 + i) * 4 * KB, [P, CW], F32R) for i in range(RAW)]
        lo = [at(f"lo{i}", RING + (8 + i) * 4 * KB, [P, CW], F32R) for i in range(LOS)]
        move = at("move", MOVE, [P, KT, 2 * T], F32R)

        misc = [MISC]

        def small(name, shape, dt=F32):
            n = int(np.prod(shape[1:])) * 4
            t = at(name, misc[0], shape, dt)
            misc[0] += -(-n // 32) * 32
            assert misc[0] <= end, name
            return t

        upper = [small(f"upper{i}", [P, T]) for i in range(2)]
        ident_at = misc[0]
        ident = small("ident", [P, P])
        ones = small("ones", [P, P])
        flip = small("flip", [P, P])
        g_mix = small("g_mix", [P, KT])
        g_ffn = small("g_ffn", [P, KT])
        sinks = small("sinks", [P, A_Q])
        neg_sinks = small("neg_sinks", [P, A_Q])
        stat = small("stat", [P, 8])
        group_max = small("group_max", [P, TT, B_G])
        one_at = misc[0]
        gate_t = small("gate_t", [P, T])
        rstd_in = nc.alloc_sbuf_tensor_at("rstd_in", [P, T], F32, offset=one_at)
        one_i = small("one_i", [P, 2, P])
        one_j = [small(f"one_j{i}", [P, 2, P]) for i in range(2)]
        zero = nc.alloc_sbuf_tensor_at("zero", [P, 512], BF16, offset=ident_at)
        iota128 = nc.alloc_sbuf_tensor_at("iota128", [P, P], F32, offset=ident_at + 2 * P * 4)
        act_hi = [at(f"act_hi{i}", one_at + i * KB, [P, T], F32R) for i in range(2)]
        act_lo = [at(f"act_lo{i}", one_at + (2 + i) * KB, [P, T], F32R) for i in range(2)]

        qk = at("qk", ARENA, [P, N_QK, T])
        v_nat = at("v_nat", ARENA + 34 * KB, [P, TT, N_V, HD])
        gates = at("gates", ARENA + 48 * KB, [P, 2 * KT, T])
        bias = at("bias", ARENA + 80 * KB, [P, HEADS, N_BIAS])
        prob = at("prob", ARENA + 110 * KB, [P, 2, B_G, T])
        prob_t = at("prob_t", ARENA + 116 * KB, [P, B_G, TT, T])
        q_now = at("q_now", ARENA + 122 * KB, [P, B_G, T])
        v_now = at("v_now", ARENA + 125 * KB, [P, TT, B_G, HD])
        v_t = [at(f"v_t{i}", ARENA + (116 + i) * KB, [P, T]) for i in range(2)]
        x_t = at("x_t", ARENA + 48 * KB, [P, KT, T])
        x_sq = at("x_sq", ARENA + 64 * KB, [P, KT, T])
        rows_sb = at("rows_sb", ARENA + 116 * KB, [N_ROWS, N_DELTA])
        table_sb = at("table_sb", ARENA + 118 * KB, [N_ROWS, HEADS])
        line_sb = at("line_sb", ARENA + 110 * KB, [HEADS, N_DELTA])
        ssq = at("ssq", ARENA + 122 * KB, [P, T])
        ssq_b = at("ssq_b", ARENA + 126 * KB, [P, T])
        mean = at("mean", ARENA + 123 * KB, [P, T])
        rstd = at("rstd", ARENA + 124 * KB, [P, T])
        work = at("work", ARENA + 125 * KB, [P, T])
        hankel = at("hankel", ARENA + 48 * KB, [P, HEADS, N_BIAS])
        att = at("att", ARENA + 80 * KB, [P, A_Q + B_S, 2 * T], F32R)
        merged = [at(f"merged{i}", ARENA + (104 + i) * KB, [P, T]) for i in range(4)]
        x_again = at("x_again", ARENA, [P, KT, T])
        x1 = at("x1", ARENA + 16 * KB, [P, KT, T])
        sq1 = [at(f"sq1{i}", ARENA + (108 + i) * KB, [P, T]) for i in range(2)]
        h2 = at("h2", ARENA + 48 * KB, [P, KT, T])
        x1_nat = at("x1_nat", ARENA + 64 * KB, [P, TT, D])
        keys_sb = at("keys_sb", ARENA + 80 * KB, [P, HC, NK])
        query = [at(f"query{i}", ARENA + (88 + i) * KB, [P, T]) for i in range(2)]
        score = [at(f"score{i}", ARENA + (90 + i) * KB, [P, TT, NK]) for i in range(2)]
        score_b = at("score_b", ARENA + 92 * KB, [P, TT, NK])
        top_now = [at(f"top_now{i}", ARENA + 94 * KB + i * 128, [P, TT, TOPK]) for i in range(2)]
        idx_now = [at(f"idx_now{i}", ARENA + 94 * KB + 256 + i * 128, [P, TT, TOPK], U32) for i in range(2)]
        top_s = at("top_s", ARENA + 100 * KB, [P, TT, PH, 2, TOPK])
        top_i = at("top_i", ARENA + 102 * KB, [P, TT, PH, 2, TOPK])
        cand = at("cand", ARENA + 104 * KB, [P, TOPK * TOPK])
        cand_b = at("cand_b", ARENA + 105 * KB, [P, TOPK * TOPK])
        pick = at("pick", ARENA + 106 * KB, [P, 2, TOPK, TOPK])
        pick_b = at("pick_b", ARENA + 114 * KB, [P, 2, TOPK, TOPK])
        best_s = at("best_s", ARENA + 108 * KB, [P, TOPK])
        best_j = at("best_j", ARENA + 108 * KB + 64, [P, TOPK], U32)
        half_u = at("half_u", ARENA + 108 * KB + 128, [P, 2, TOPK], U32)
        half_f = at("half_f", ARENA + 108 * KB + 256, [P, 2, TOPK])
        soft_sum = at("soft_sum", ARENA + 108 * KB + 448, [P, TT * PH])
        iota16 = at("iota16", ARENA + 113 * KB, [P, TOPK])
        found_ij = at("found_ij", ARENA + 109 * KB, [P, 2, TT, PH * TOPK])
        found_g = at("found_g", ARENA + 111 * KB, [P, TT, PH * TOPK])
        act = at("act", ARENA, [P, NK, T])
        x2 = at("x2", MOVE + 14 * KB, [P, TT, D])
        g_final = at("g_final", ARENA, [P, D])
        squares = at("squares", ARENA + 8 * KB, [P, D])
        y = at("y", ARENA + 16 * KB, [P, TT, D])

        ps = [ctx.enter_context(nc.psum_tensor(f"ps{i}", [P, 512], F32)) for i in range(8)]

        line_dram = nc.dram_tensor("line_scratch", [HEADS * N_DELTA], F32)
        x1_dram = nc.dram_tensor("x1_scratch", [P, TT * D], F32)

        small_in, g_in, const_in, x_in = sem("small_in"), sem("g_in"), sem("const_in"), [sem(f"x_in{q}") for q in range(4)]
        keys_in, x_again_in, bias_in = sem("keys_in"), sem("x_again_in"), sem("bias_in")
        raw_landed = [sem(f"raw_landed{i}") for i in range(RAW)]
        hi_ready = sem("hi_ready")
        lo_ready = sem("lo_ready")
        chunk_used = sem("chunk_used")
        upper_ready = sem("upper_ready")
        block_summed = sem("block_summed")
        dve_step = sem("dve_step")
        consts = sem("consts")
        settled = sem("settled")
        line_sum, line_ready, line_out = sem("line_sum"), sem("line_ready"), sem("line_out")
        bias_flipped, bias_ready = sem("bias_flipped"), sem("bias_ready")
        sq_ready, ssq_ready, ssq_sum = sem("sq_ready"), sem("ssq_ready"), sem("ssq_sum")
        inv_ready, root_ready = sem("inv_ready"), sem("root_ready")
        x_hi, halves_added = sem("x_hi"), sem("halves_added")
        norm_ready, norm_hi, move_ready = sem("norm_ready"), sem("norm_hi"), sem("move_ready")
        vt_turned, vn_ready = sem("vt_turned"), sem("vn_ready")
        q_staged, v_staged = sem("q_staged"), sem("v_staged")
        scores_done, max_ready, exp_done, prob_ready = (
            sem("scores_done"), sem("max_ready"), sem("exp_done"), sem("prob_ready"))
        prob_turned, prob_copied, pv_done, o_ready = (
            sem("prob_turned"), sem("prob_copied"), sem("pv_done"), sem("o_ready"))
        att_hi, att_ready, bias_used = sem("att_hi"), sem("att_ready"), sem("bias_used")
        sig_ready, gated_a, gated_b = sem("sig_ready"), sem("gated_a"), sem("gated_b")
        merged_ready, merged_hi, merged_lo = sem("merged_ready"), sem("merged_hi"), sem("merged_lo")
        x1_ready, x1_sq, sq_added = sem("x1_ready"), sem("x1_sq"), sem("sq_added")
        x1_turned, x1_copied, x1_out = sem("x1_turned"), sem("x1_copied"), sem("x1_out")
        key_scores, score_ready, top_ready, top_kept = (
            sem("key_scores"), sem("score_ready"), sem("top_ready"), sem("top_kept"))
        best_ready, soft_ready, found_ready = sem("best_ready"), sem("soft_ready"), sem("found_ready")
        picked, picked_row = sem("picked"), sem("picked_row")
        iota_ready, found_turned, experts_ready = sem("iota_ready"), sem("found_turned"), sem("experts_ready")
        act_ready, move_free = sem("act_ready"), sem("move_free")
        one_i_ready, one_j_ready, gates_spread, gated = (
            sem("one_i_ready"), sem("one_j_ready"), sem("gates_spread"), sem("gated"))
        one_j_gated, act_ones, multiplied = sem("one_j_gated"), sem("act_ones"), sem("multiplied")
        act_hi_ready, act_lo_ready = sem("act_hi_ready"), sem("act_lo_ready")
        zero_ready, down_done = sem("zero_ready"), sem("down_done")
        x2_in, g_final_in, x2_ready, x2_sq, y_ready, y_out = (
            sem("x2_in"), sem("g_final_in"), sem("x2_ready"), sem("x2_sq"), sem("y_ready"), sem("y_out"))

        block = ctx.enter_context(nc.Block())

        def flat(ap):
            return ap.rearrange("p a t -> p (a t)")

        def pick1(t, i):
            return flat(t[:, bass.ds(i, 1), :])

        @block.sync
        def _(sp):
            def load(name, it, s, first=False):
                c = CHUNK0[name] + BODY * it + s
                if not first:
                    sp.wait_ge(lo_ready, c - RAW + 1)
                src = A["w_" + name][bass.ds(BODY * it + s, 1), :, :].rearrange("a p n -> p (a n)")
                sp.dma_start(raw[s][:], src).then_inc(raw_landed[s], 16)

            sp.dma_start(g_mix[:], A["g_mix"]).then_inc(g_in, 16)
            for q in range(4):
                sp.dma_start(x_t[:, 4 * q:4 * q + 4, :], A["x_t"][:, 4 * q:4 * q + 4, :]).then_inc(x_in[q], 16)
            load("qk", 0, 0, first=True)
            load("qk", 0, 1, first=True)
            sp.dma_start(rows_sb[:], A["bias_rows"]).then_inc(small_in, 16)
            sp.dma_start(table_sb[0:N_BUCKETS, :], A["rel_bias"]).then_inc(small_in, 16)
            sp.dma_start(table_sb[N_BUCKETS:N_ROWS, :], A["head_kinds"]).then_inc(small_in, 16)
            load("qk", 0, 2, first=True)
            load("qk", 0, 3, first=True)
            sp.dma_start(flip[:], A["flip"]).then_inc(const_in, 16)
            sp.dma_start(ident[:], A["ident"]).then_inc(const_in, 16)
            sp.dma_start(g_ffn[:], A["g_ffn"]).then_inc(const_in, 16)
            sp.dma_start(sinks[:], spread(A["sink_a"], A_Q)).then_inc(const_in, 16)
            sp.wait_ge(line_ready, 1)
            sp.dma_start(line_dram.ap().rearrange("(h m) -> h m", h=HEADS), line_sb[:]).then_inc(line_out, 16)
            for s in range(BODY):
                load("qk", 1, s)
            sp.wait_ge(line_out, 16)
            sp.wait_ge(move_ready, 4)
            sp.wait_ge(ssq_ready, 2)
            for n in range(HEADS // SLANT):
                sp.dma_start(hankel[:, n * SLANT:(n + 1) * SLANT, :], slant(line_dram, n * SLANT, SLANT)
                             ).then_inc(bias_in, 16)
                for s in range(BODY):
                    load("qk", n + 2, s)
            with sp.Fori(HEADS // SLANT + 2, CHUNKS["qk"] // BODY) as it:
                for s in range(BODY):
                    load("qk", it, s)
            for name in ("v", "gate", "oa", "ob"):
                with sp.Fori(0, CHUNKS[name] // BODY) as it:
                    for s in range(BODY):
                        load(name, it, s)
                if name == "oa":
                    sp.wait_ge(att_ready, 4)
                    sp.dma_start(x_again[:], A["x_t"]).then_inc(x_again_in, 16)
            with sp.Fori(0, CHUNKS["out"] // BODY) as it:
                for s in range(BODY):
                    load("out", it, s)
            for s in range(BODY):
                load("pq", 0, s)
            sp.wait_ge(merged_lo, KT + 4)
            sp.dma_start(keys_sb[:], A["keys"]).then_inc(keys_in, 16)
            sp.wait_ge(x1_copied, 8)
            sp.dma_start(x1_dram.ap(), x1_nat[:].rearrange("p a d -> p (a d)")).then_inc(x1_out, 16)
            with sp.Fori(1, CHUNKS["pq"] // BODY) as it:
                for s in range(BODY):
                    load("pq", it, s)
            with sp.Fori(0, CHUNKS["u"] // BODY) as it:
                for s in range(BODY):
                    load("u", it, s)
            for s in range(BODY):
                load("down", 0, s)
            sp.wait_ge(x1_out, 16)
            sp.wait_ge(move_free, 1)
            sp.dma_start(x2[:].rearrange("p a d -> p (a d)"), x1_dram.ap()).then_inc(x2_in, 16)
            with sp.Fori(1, CHUNKS["down"] // BODY // 2) as it:
                for s in range(BODY):
                    load("down", it, s)
            sp.wait_ge(act_lo_ready, 40)
            sp.dma_start(g_final[:], spread(A["g_final"], D)).then_inc(g_final_in, 16)
            with sp.Fori(CHUNKS["down"] // BODY // 2, CHUNKS["down"] // BODY) as it:
                for s in range(BODY):
                    load("down", it, s)
            for n in range(2 * TT):
                sp.wait_ge(y_ready, n + 1)
                tt, half = n // 2, slice(n % 2 * D // 2, (n % 2 + 1) * D // 2)
                sp.dma_start(out[tt * P:(tt + 1) * P, half], y[:, tt, half]).then_inc(y_out, 16)
            sp.wait_ge(y_out, 16 * 2 * TT)

        @block.gpsimd
        def _(pool):
            for q in range(4):
                part = x_t[:, 4 * q:4 * q + 4, :]
                pool.wait_ge(x_in[q], 16)
                nc.gpsimd.tensor_tensor(x_sq[:, 4 * q:4 * q + 4, :], part, part, ALU.mult).then_inc(sq_ready, 1)
            pool.wait_ge(block_summed, BLOCK0["v"] + 2)
            with pool.Fori(0, A_Q) as h:
                pool.wait_ge(scores_done, h + 1)
                nc.gpsimd.tensor_copy(q_now[:, 0, :], pick1(qk, h)).then_inc(q_staged, 1)
            with pool.Fori(0, B_S) as s:
                pool.wait_ge(scores_done, s + A_Q + 1)
                heads = qk[:, A_Q:A_Q + B_H, :].rearrange("p (g s) t -> p g s t", s=B_S)
                nc.gpsimd.tensor_copy(q_now[:], heads[:, :, bass.ds(s, 1), :].rearrange("p g a t -> p g (a t)")
                                      ).then_inc(q_staged, 1)
                pool.wait_ge(vn_ready, N_V + 2)
                pool.wait_ge(pv_done, s + A_Q)
                for tt in range(TT):
                    vs = v_nat[:, tt, A_KV:, :].rearrange("p (g s) d -> p g s d", s=B_S)
                    nc.gpsimd.tensor_copy(v_now[:, tt, :, :], vs[:, :, bass.ds(s, 1), :].rearrange("p g a d -> p g (a d)")
                                          ).then_inc(v_staged, 1)
            pool.wait_ge(gated_a, KT + 2)
            with pool.Fori(0, KT // 4) as it:
                for e in range(4):
                    n = it * 4 + e
                    pool.wait_ge(block_summed, n + BLOCK0["ob"] + 3)
                    pool.wait_ge(sig_ready, KT)
                    nc.gpsimd.tensor_tensor(merged[e][:], merged[e][:], pick1(gates, n + KT), ALU.mult).then_inc(gated_b, 1)
                    pool.wait_ge(gated_b, n + 1)
                    nc.gpsimd.tensor_tensor(merged[e][:], merged[e][:], pick1(gates, n), ALU.add).then_inc(merged_ready, 1)
            nc.gpsimd.iota(iota16[:], [[1, TOPK]], base=0, channel_multiplier=0,
                           allow_small_or_imprecise_dtypes=True).then_inc(iota_ready, 1)
            pool.wait_ge(move_ready, 8)
            pool.wait_ge(x1_out, 16)
            nc.gpsimd.memset(act[:, J_KEPT:80, :], 1.0).then_inc(act_ones, 1)
            nc.gpsimd.memset(act[:, 116:NK, :], 1.0).then_inc(act_ones, 1)
            rows = top_i[:].rearrange("p t h c k -> p (t h) c k")
            pool.wait_ge(top_kept, HC + 2)
            with pool.Fori(0, TT * PH) as it:
                pool.wait_ge(picked, it + 1)
                r = rows[:, bass.ds(it, 1), :, :].rearrange("p a c k -> p (a c) k").unsqueeze(2).to_broadcast([P, 2, TOPK, TOPK])
                nc.gpsimd.tensor_tensor(pick_b[:], pick[:], r, ALU.mult).then_inc(picked_row, 1)
                nc.gpsimd.tensor_copy(pick1(act, it + 80).rearrange("p (a t) -> p a t", a=TT),
                                      ones[:].unsqueeze(1).to_broadcast([P, TT, P])).then_inc(act_ones, 1)
            pool.wait_ge(found_turned, 3)
            nc.gpsimd.iota(iota128[:], [[1, P]], base=0, channel_multiplier=0,
                           allow_small_or_imprecise_dtypes=True).then_inc(iota_ready, 1)
            nc.gpsimd.memset(act[:, 96:116, :], 1.0).then_inc(act_ones, 1)
            pool.wait_ge(act_ones, TT * PH + 3)
            nc.gpsimd.memset(zero[:], 0.0).then_inc(zero_ready, 1)
            pool.wait_ge(experts_ready, 1)
            with pool.Fori(0, PAIRS // BODY) as it:
                for s in range(BODY):
                    pool.wait_ge(one_j_ready, it * BODY + (s + 1))
                    g = gate_t[:, bass.ds(it * 2 * BODY + 2 * s, 2)].unsqueeze(2).to_broadcast([P, 2, P])
                    nc.gpsimd.tensor_tensor(one_j[s % 2][:], one_j[s % 2][:], g, ALU.mult).then_inc(one_j_gated, 1)

        @block.scalar
        def _(a):
            def hi_of(cb, it, s):
                slot = s % RAW
                a.wait_ge(raw_landed[slot], it * 16 + (cb // 4 + s // 4) * 16 + 16)
                a.wait_ge(chunk_used, it * BODY + cb + s + 1)
                nc.scalar.copy(hi[slot][:], raw[slot][:]).then_inc(hi_ready, 1)

            def upper_of(b, e, used, multiplied_to=None, bank=None):
                a.wait_ge(chunk_used, used + RAW)
                if multiplied_to is not None:
                    a.wait_ge(multiplied, multiplied_to)
                a.wait_ge(block_summed, b + 1)
                nc.scalar.copy(upper[e][:], ps[e if bank is None else bank][:, T:2 * T]).then_inc(upper_ready, 1)

            def body(name, it, after=None, used_by=None):
                c0, b0 = CHUNK0[name], BLOCK0[name]
                for s in range(BODY):
                    hi_of(c0, it, s + 2)
                    if name == "oa":
                        upper_of(it * 4 + b0 + s, s % 2, it * BODY + c0 + s + 1)
                    elif name == "ob":
                        for e in range(2):
                            upper_of(it * 8 + b0 + 2 * s + e, e, it * BODY + c0 + s + 1, bank=((s + 1) % 2) * 2 + e)
                    elif s % 2:
                        upper_of(it * 2 + b0 + s // 2, s // 2, it * BODY + c0 + s + 1,
                                 it * 2 + s // 2 - J_KEPT + 1 if used_by else None)
                    if after:
                        after(it, s)

            for ring in (vn_ready, score_ready, top_kept):
                a.sem_inc(ring, 2)
            a.sem_inc(o_ready, 1)

            a.wait_ge(g_in, 16)
            for k in range(KT):
                if k % 4 == 0:
                    a.wait_ge(x_in[k // 4], 16)
                if k == 8:
                    hi_of(0, 0, 0)
                nc.scalar.activation(move[:, k, 0:T], x_t[:, k, :], ACT.Copy, scale=g_mix[:, k:k + 1]).then_inc(x_hi, 1)
            hi_of(0, 0, 1)
            a.sem_inc(bias_ready, 2)

            def line_and_root(it, s):
                if s == 0:
                    a.wait_ge(line_sum, 1)
                    nc.scalar.copy(line_sb[:], ps[6][0:HEADS, :]).then_inc(line_ready, 1)
                if s == 2:
                    a.wait_ge(inv_ready, 1)
                    nc.scalar.activation(rstd_in[:], work[:], ACT.Sqrt).then_inc(root_ready, 1)

            def keep_bias(it, s):
                if s % 2:
                    h = (it - FLIP0) * 2 + s // 2
                    a.wait_ge(bias_flipped, h + 1)
                    nc.scalar.copy(pick1(bias, h), ps[6 + s // 2][:, 0:N_BIAS]).then_inc(bias_ready, 1)
            body("qk", 0, line_and_root)
            with a.Fori(1, FLIP0) as it:
                body("qk", it)
            with a.Fori(FLIP0, CHUNKS["qk"] // BODY) as it:
                body("qk", it, keep_bias)

            def keep_v(it, s):
                if s % 2:
                    n, e = it * 2 + s // 2, s // 2 % 2
                    a.wait_ge(vt_turned, n + 3)
                    nc.scalar.copy(v_nat[:, :, bass.ds(n, 1), :].rearrange("p t a d -> p t (a d)"),
                                   ps[6 + e][:, 0:T].rearrange("p (t d) -> p t d", t=TT)).then_inc(vn_ready, 1)
            left = run(a, body, "v", (keep_v, 3), carry=True)

            def heads_a(h, s):
                if s == 0:
                    a.wait_ge(max_ready, h + 1)
                    for u in range(2):
                        nc.scalar.activation(prob[:, u, 0, :], prob[:, u, 0, :], ACT.Exp, bias=stat[:, u:u + 1],
                                             accum_out=stat[:, 2 + u:3 + u]).then_inc(exp_done, 1)
                    nc.scalar.activation(stat[:, 4:6], stat[:, 0:2], ACT.Exp, bias=sinks[:, bass.ds(h, 1)]
                                         ).then_inc(exp_done, 1)
                if s == 2:
                    a.wait_ge(prob_turned, h + 2)
                    nc.scalar.copy(prob_t[:, 0, :, :], ps[3][:].rearrange("p (k q) -> p k q", k=TT)).then_inc(prob_copied, 1)
                if s == 3:
                    a.wait_ge(pv_done, h + 1)
                    nc.scalar.copy(pick1(qk, h), ps[5][:, 0:T]).then_inc(o_ready, 1)
            body("gate", 0, lambda h, s: (carried_out(left, s), heads_a(h, s)))
            with a.Fori(1, A_Q) as h:
                body("gate", h, heads_a)

            def slot(s4, last=False):
                def heads_b(half):
                    def f(it, s):
                        if last and half == 1 and s < 3:
                            lo_, hi_ = ATT_PARTS[s]
                            if s == 0:
                                a.wait_ge(bias_used, 1)
                            nc.scalar.copy(att[:, lo_:hi_, 0:T], qk[:, lo_:hi_, :]).then_inc(att_hi, 1)
                        if half == 0 and s == 3:
                            a.wait_ge(max_ready, s4 + A_Q + 1)
                            for u in range(2):
                                nc.scalar.activation(prob[:, u, :, :], prob[:, u, :, :], ACT.Exp, bias=stat[:, u:u + 1],
                                                     accum_out=stat[:, 2 + u:3 + u]).then_inc(exp_done, 1)
                        if half == 1 and s == 2:
                            a.wait_ge(prob_turned, s4 + A_Q + 2)
                            for g in range(B_G):
                                nc.scalar.copy(prob_t[:, g, :, :], ps[2 + g][:].rearrange("p (k q) -> p k q", k=TT)
                                               ).then_inc(prob_copied, 1)
                        if half == 1 and s == 3:
                            a.wait_ge(pv_done, s4 + A_Q + 1)
                            nc.scalar.copy(pick1(qk, s4 + A_Q), ps[5][:, 0:T]).then_inc(o_ready, 1)
                    return f
                body("gate", s4 * 2 + A_Q, heads_b(0))
                body("gate", s4 * 2 + A_Q + 1, heads_b(1))
            with a.Fori(0, B_S - 1) as s4:
                slot(s4)
            a.wait_ge(o_ready, A_Q + B_S)
            slot(B_S - 1, last=True)
            a.wait_ge(o_ready, A_Q + B_S + 1)
            nc.scalar.copy(att[:, A_Q + B_S - 1, 0:T], qk[:, A_Q + B_S - 1, :]).then_inc(att_hi, 1)

            def gate(it, s):
                n = it * 4 + s + 2
                both = gates[:].rearrange("p (k n) t -> p k n t", k=2)[:, :, bass.ds(n, 1), :].rearrange("p k a t -> p k (a t)")
                nc.scalar.activation(both, both, ACT.Sigmoid).then_inc(sig_ready, 1)
            a.wait_ge(block_summed, BLOCK0["gate"] + KT + 2 + 2)
            gate(0, -2)
            gate(0, -1)
            with a.Fori(0, CHUNKS["oa"] // BODY - 1) as it:
                body("oa", it, gate)
            body("oa", CHUNKS["oa"] // BODY - 1, lambda it, s: gate(it, s) if s < 2 else None)

            def keep_merged(it, s):
                for e in range(2):
                    n = it * 8 + 2 * s + e
                    a.wait_ge(merged_ready, n + 1)
                    nc.scalar.copy(move[:, bass.ds(n, 1), 0:T].rearrange("p a t -> p (a t)"), merged[s % 2 * 2 + e][:]
                                   ).then_inc(merged_hi, 1)
            left = run(a, body, "ob", (keep_merged, 1), carry=True)

            def square(it, s):
                if s % 2:
                    n = it * 2 + s // 2
                    a.wait_ge(x1_ready, n + 1)
                    a.wait_ge(sq_added, n + 1)
                    nc.scalar.activation(sq1[s // 2 % 2][:], pick1(x1, n), ACT.Square).then_inc(x1_sq, 1)
            run(a, body, "out", (square, 1), carried=left)

            def turned(n):
                a.wait_ge(x1_turned, n + 1)
                nc.scalar.copy(x1_nat[:, n // 4, (n % 4) * 512:(n % 4) * 512 + 512], ps[TURN_BANKS[n % TURNS]][:]
                               ).then_inc(x1_copied, 1)
            a.wait_ge(inv_ready, 2)
            nc.scalar.activation(rstd[:], work[:], ACT.Sqrt).then_inc(root_ready, 1)
            for n in range(4):
                turned(n)
            for q in range(4):
                a.wait_ge(norm_ready, 4 * q + 4)
                nc.scalar.copy(move[:, 4 * q:4 * q + 4, 0:T], h2[:, 4 * q:4 * q + 4, :]).then_inc(norm_hi, 1)
                turned(4 + q)

            def keep_scores(it, s):
                if s % 2:
                    n, e = it * 2 + s // 2, s // 2 % 2
                    a.wait_ge(key_scores, n + 3)
                    a.wait_ge(top_ready, n + 1)
                    nc.scalar.copy(score[e][:], ps[6 + e][:, 0:T].rearrange("p (t k) -> p t k", t=TT)).then_inc(score_ready, 1)

            def keep_top(it, s):
                if s % 2:
                    n, e = it * 2 + s // 2, s // 2 % 2
                    a.wait_ge(top_ready, n + 3)
                    nc.scalar.copy(top_s[:].rearrange("p t h c k -> p t (h c) k")[:, :, bass.ds(n, 1), :]
                                   .rearrange("p t a k -> p t (a k)"), top_now[e][:])
                    nc.scalar.copy(top_i[:].rearrange("p t h c k -> p t (h c) k")[:, :, bass.ds(n, 1), :]
                                   .rearrange("p t a k -> p t (a k)"), idx_now[e][:]).then_inc(top_kept, 1)
            left = run(a, body, "pq", (keep_scores, 3), (keep_top, 4), carry=True)

            def gelu_of(j, e, dst):
                a.wait_ge(block_summed, j + BLOCK0["u"] + 3)
                nc.scalar.activation(dst, upper[e][:], ACT.Gelu).then_inc(act_ready, 1)

            def gelu_kept(it, s):
                if s == 0:
                    gelu_of(it * 2 - 1, 1, pick1(act, it * 2 - 1))
                if s == 2:
                    gelu_of(it * 2, 0, pick1(act, it * 2))
            a.wait_ge(x1_out, 16)
            body("u", 0, lambda it, s: (carried_out(left, s), gelu_kept(it, s) if s else None))
            with a.Fori(1, UR) as it:
                body("u", it, gelu_kept)
            a.wait_ge(best_ready, UR)
            nc.scalar.activation(found_g[:], found_g[:], ACT.Exp).then_inc(soft_ready, 1)

            def gelu_and_gates(it, s):
                gelu_kept(it, s)
                if s == 2:
                    a.wait_ge(found_turned, 3)
                    nc.scalar.copy(gate_t[:], ps[4][:, 0:T]).then_inc(experts_ready, 1)
            body("u", UR, gelu_kept)
            body("u", UR + 1, gelu_and_gates)

            def gelu(it, s):
                if s == 0:
                    gelu_of(it * 2 - 1, 1, upper[1][:])
                if s == 2:
                    gelu_of(it * 2, 0, upper[0][:])
            with a.Fori(U0, CHUNKS["u"] // BODY) as it:
                body("u", it, gelu, used_by=multiplied)
            gelu_of(NK - 1, 1, upper[1][:])

            def act_hi_of(j, r):
                a.wait_ge(chunk_used, j * 2 + CHUNK0["down"] - 2 + RAW)
                nc.scalar.copy(act_hi[r][:], pick1(act, j)).then_inc(act_hi_ready, 1)

            a.wait_ge(gated, PAIRS + 2)
            act_hi_of(0, 0)

            def down(it, last=False):
                c0 = CHUNK0["down"]
                for s in range(BODY):
                    if not (last and s >= 2):
                        hi_of(c0, it, s + 2)
                    if s % 2 == 0 and not (last and s == 2):
                        act_hi_of(it * 2 + s // 2 + 1, (s // 2 + 1) % 2)
            with a.Fori(0, CHUNKS["down"] // BODY - 1) as it:
                down(it)
            down(CHUNKS["down"] // BODY - 1, last=True)

            for tt in range(TT):
                a.wait_ge(x2_ready, 4 * tt + 4)
                if tt:
                    a.wait_ge(x2_sq, tt)
                nc.scalar.activation(squares[:], x2[:, tt, :], ACT.Square, accum_out=stat[:, tt:tt + 1]).then_inc(x2_sq, 1)
                a.wait_ge(inv_ready, 3 + tt)
                nc.scalar.activation(stat[:, 4 + tt:5 + tt], stat[:, 2 + tt:3 + tt], ACT.Sqrt).then_inc(root_ready, 1)

        @block.vector
        def _(v):
            me = Steps(v, dve_step)
            did, wait = me.did, me.wait

            def lo_of(cb, it, s):
                v.wait_ge(hi_ready, it * BODY + cb + s + 1)
                v.wait_ge(chunk_used, it * BODY + cb + s - LOS + 1 + RAW)
                nc.vector.tensor_tensor(lo[s % LOS][:], raw[s % RAW][:], hi[s % RAW][:].bitcast(F32), ALU.subtract
                                        ).then_inc(lo_ready, 1)

            def sum_of(b, bank, dst, up=None):
                v.wait_ge(upper_ready, b + 1)
                nc.vector.tensor_tensor(dst, ps[bank][:, 0:T], upper[bank if up is None else up][:], ALU.add
                                        ).then_inc(block_summed, 1)

            def normed_sum_of(b, bank, dst):
                v.wait_ge(upper_ready, b + 1)
                nc.vector.tensor_tensor(upper[bank][:], ps[bank][:, 0:T], upper[bank][:], ALU.add).then_inc(halves_added, 1)
                v.wait_ge(halves_added, b + 1)
                nc.vector.tensor_tensor(dst, upper[bank][:], rstd_in[:], ALU.mult).then_inc(block_summed, 1)

            def rsqrt_of(m, w, r, n):
                nc.vector.reciprocal(w, m).then_inc(inv_ready, 1)
                v.wait_ge(root_ready, n)
                for o, x0, x1_ in ((w, r, r), (w, w, m)):
                    did(nc.vector.tensor_tensor(o, x0, x1_, ALU.mult))
                    wait()
                did(nc.vector.tensor_scalar(w, w, -0.5, 1.5, ALU.mult, ALU.add))
                wait()
                did(nc.vector.tensor_tensor(r, r, w, ALU.mult))
                wait()

            def normed(src, dst, g):
                def scale(q):
                    for k in range(4 * q, 4 * q + 4):
                        nc.vector.scalar_tensor_tensor(out=dst[:, k, :], in0=src[:, k, :], scalar=g[:, k:k + 1],
                                                       in1=rstd[:], op0=ALU.mult, op1=ALU.mult).then_inc(norm_ready, 1)

                def split(q):
                    v.wait_ge(norm_hi, q + 1)
                    nc.vector.tensor_tensor(move[:, 4 * q:4 * q + 4, T:2 * T], dst[:, 4 * q:4 * q + 4, :],
                                            move[:, 4 * q:4 * q + 4, 0:T].bitcast(F32), ALU.subtract).then_inc(move_ready, 1)
                scale(0)
                scale(1)
                split(0)
                split(1)
                scale(2)
                scale(3)
                split(2)
                split(3)

            def settle():
                v.sem_inc(settled, 1)

            def body(name, it, after=None):
                for s in range(BODY):
                    lo_of(CHUNK0[name], it, s + 1)
                    if after:
                        after(it, s)

            v.sem_inc(block_summed, 2)
            v.sem_inc(top_ready, 2)
            v.sem_inc(gated_a, 2)
            v.sem_inc(merged_lo, 4)
            v.sem_inc(sq_added, 2)
            v.sem_inc(gated, 2)
            v.sem_inc(multiplied, 2)

            nc.vector.memset(ones[:], 1.0).then_inc(consts, 1)
            v.wait_ge(g_in, 16)
            for k in range(KT):
                v.wait_ge(x_hi, k + 1)
                ins = nc.vector.scalar_tensor_tensor(out=move[:, k, T:2 * T], in0=x_t[:, k, :], scalar=g_mix[:, k:k + 1],
                                                     in1=move[:, k, 0:T].bitcast(F32), op0=ALU.mult, op1=ALU.subtract)
                if k % 4 == 3:
                    ins.then_inc(move_ready, 1)
                if k == 7:
                    lo_of(0, 0, 0)

            def norm1(it, s):
                if s in (-3, -2):
                    half = s + 3
                    v.wait_ge(sq_ready, 2 * half + 2)
                    nc.vector.tensor_reduce((ssq, ssq_b)[half][:], x_sq[:, 8 * half:8 * half + 8, :].rearrange("p k t -> p t k"),
                                            AX.X, ALU.add).then_inc(ssq_ready, 1)
                if s == -1:
                    v.wait_ge(ssq_sum, 1)
                    did(nc.vector.tensor_scalar(mean[:], ps[5][:, 0:T], 1.0 / D, EPS, ALU.mult, ALU.add))
                    wait()
                    rsqrt_of(mean[:], work[:], rstd_in[:], 1)

            def keep_qk(it, s):
                if s % 2:
                    n = it * 2 + s // 2
                    normed_sum_of(n + BLOCK0["qk"], s // 2 % 2, pick1(qk, n))
            left = run(v, body, "qk", (keep_qk, 1), carried=[(norm1, 3, 0)], carry=True)
            v.wait_ge(const_in, 16 * 4)
            did(nc.vector.tensor_scalar(neg_sinks[:], sinks[:], -1.0, None, ALU.mult))
            me.flat()

            def keep_vt(it, s):
                if s % 2:
                    n, e = it * 2 + s // 2, s // 2 % 2
                    v.wait_ge(vt_turned, n + 1)
                    normed_sum_of(n + BLOCK0["v"], e, v_t[e][:])
            left = run(v, body, "v", (keep_vt, 1), carried=left, carry=True)

            def biased(h, g, u, bank, off):
                did(nc.vector.scalar_tensor_tensor(
                    out=prob[:, u, g, :], in0=ps[bank][:, u * T:(u + 1) * T], scalar=SCALE,
                    in1=flat(bias[:, bass.ds(h, 1), off:off + T]), op0=ALU.mult, op1=ALU.add))

            def keep_gate(it, s):
                if s % 2:
                    n = it * 2 + s // 2
                    normed_sum_of(n + BLOCK0["gate"], s // 2 % 2, pick1(gates, n))

            def divided(n, w):
                did(nc.vector.reciprocal(stat[:, 6:8], stat[:, 2:4]))
                wait()
                for u in range(2):
                    nc.vector.tensor_scalar(prob[:, u, 0:w, :], prob[:, u, 0:w, :], stat[:, 6 + u:7 + u], None, ALU.mult
                                            ).then_inc(prob_ready, 1)

            v.wait_ge(bias_ready, HEADS + 2)
            def heads_a(h, s):
                if isinstance(h, int):
                    carried_out(left, s)
                if s or not isinstance(h, int):
                    keep_gate(h, s - 1)
                if s == 0:
                    v.wait_ge(scores_done, h + 2)
                    v.wait_ge(prob_turned, h + 1)
                    for u in range(2):
                        biased(h, 0, u, 2, P - u * P)
                    wait()
                    did(nc.vector.tensor_reduce(stat[:, 0:2], prob[:, :, 0, :], AX.X, ALU.max, negate=True))
                    wait()
                    nc.vector.tensor_scalar(stat[:, 0:2], stat[:, 0:2], neg_sinks[:, bass.ds(h, 1)], None, ALU.min
                                            ).then_inc(max_ready, 1)
                if s == 1:
                    v.wait_ge(exp_done, h * 3 + 3)
                    did(nc.vector.tensor_tensor(stat[:, 2:4], stat[:, 2:4], stat[:, 4:6], ALU.add))
                    wait()
                    divided(h, 1)
            body("gate", 0, heads_a)
            me.flat()
            with v.Fori(1, A_Q) as h:
                me.loop(h, 5, 1)
                body("gate", h, heads_a)
            me.end_loop(A_Q - 1)

            def slot(s4, last=False):
                def heads_b(half):
                    def f(it, s):
                        if half == 0 and s < 3:
                            if s == 0:
                                v.wait_ge(scores_done, s4 + A_Q + 2)
                                v.wait_ge(prob_turned, s4 + A_Q + 1)
                            for u in range(2):
                                biased(s4 + (A_Q + s * B_S), s, u, 2 + s, P - u * P)
                            wait()
                            did(nc.vector.tensor_reduce(group_max[:, :, s], prob[:, :, s, :], AX.X, ALU.max))
                        if half == 0 and s == 2:
                            wait()
                            nc.vector.tensor_reduce(stat[:, 0:2], group_max[:], AX.X, ALU.max, negate=True
                                                    ).then_inc(max_ready, 1)
                            if last:
                                v.sem_inc(bias_used, 1)
                        if half == 1 and s == 0:
                            v.wait_ge(exp_done, s4 * 2 + 3 * A_Q + 2)
                            divided(s4, B_G)
                        keep_gate(it, s - 1)
                        if last and half == 1 and s > 0:
                            split_att(s - 1)
                    return f
                body("gate", s4 * 2 + A_Q, heads_b(0))
                body("gate", s4 * 2 + A_Q + 1, heads_b(1))

            def split_att(n):
                lo_, hi_ = ATT_PARTS[n]
                v.wait_ge(att_hi, n + 1)
                nc.vector.tensor_tensor(att[:, lo_:hi_, T:2 * T], qk[:, lo_:hi_, :], att[:, lo_:hi_, 0:T].bitcast(F32),
                                        ALU.subtract).then_inc(att_ready, 1)
            with v.Fori(0, B_S - 1) as s4:
                me.loop(s4, 10)
                slot(s4)
            me.end_loop(B_S - 1)
            slot(B_S - 1, last=True)
            me.flat()

            def gate_a(it, s):
                n, e = it * 4 + s, s % 2
                v.wait_ge(gated_a, n + 1)
                sum_of(n + BLOCK0["oa"], e, merged[e][:])
                v.wait_ge(block_summed, n + BLOCK0["oa"] + 3)
                v.wait_ge(sig_ready, n + 1)
                nc.vector.tensor_tensor(pick1(gates, n), merged[e][:], pick1(gates, n), ALU.mult).then_inc(gated_a, 1)
            left = [(keep_gate, 1, N_GATE // 2), (lambda it, s: split_att(3), 1, 0)]
            left = run(v, body, "oa", (gate_a, 1), carried=left, carry=True)

            def gate_b(it, s):
                for e in range(2):
                    n = it * 8 + (2 * s + e)
                    m = merged[s % 2 * 2 + e]
                    v.wait_ge(merged_lo, n + 1)
                    if isinstance(n, int) and n == 0:
                        v.wait_ge(gated_a, KT + 2)
                    sum_of(n + BLOCK0["ob"], ((s + 1) % 2) * 2 + e, m[:], up=e)

            def split_b(it, s):
                for e in range(2):
                    n = it * 8 + (2 * s + e)
                    v.wait_ge(merged_hi, n + 1)
                    nc.vector.tensor_tensor(move[:, bass.ds(n, 1), T:2 * T].rearrange("p a t -> p (a t)"),
                                            merged[s % 2 * 2 + e][:],
                                            move[:, bass.ds(n, 1), 0:T].rearrange("p a t -> p (a t)").bitcast(F32),
                                            ALU.subtract).then_inc(merged_lo, 1)
            left = run(v, body, "ob", (gate_b, 1), (split_b, 2), carried=left, carry=True)

            nc.vector.memset(ssq[:], 0.0).then_inc(ssq_ready, 1)
            v.wait_ge(ssq_ready, 3)
            v.wait_ge(x_again_in, 16)
            def keep_x1(it, s):
                if s % 2:
                    n = it * 2 + s // 2
                    sum_of(n + BLOCK0["out"], s // 2 % 2, pick1(x1, n))
                    v.wait_ge(block_summed, n + BLOCK0["out"] + 3)
                    nc.vector.tensor_tensor(pick1(x1, n), pick1(x1, n), pick1(x_again, n), ALU.add).then_inc(x1_ready, 1)

            def add_square(it, s):
                if s % 2:
                    n = it * 2 + s // 2
                    v.wait_ge(x1_sq, n + 1)
                    v.wait_ge(sq_added, n + 2)
                    nc.vector.tensor_tensor(ssq[:], ssq[:], sq1[s // 2 % 2][:], ALU.add).then_inc(sq_added, 1)
            run(v, body, "out", (keep_x1, 1), (add_square, 2), carried=left)
            v.wait_ge(ssq_sum, 2)
            did(nc.vector.tensor_scalar(mean[:], ps[5][:, 0:T], 1.0 / D, EPS, ALU.mult, ALU.add))
            wait()
            rsqrt_of(mean[:], work[:], rstd[:], 2)
            normed(x1, h2, g_ffn)
            me.flat()

            def keep_query(it, s):
                if s % 2:
                    n, e = it * 2 + s // 2, s // 2 % 2
                    v.wait_ge(key_scores, n + 1)
                    sum_of(n + BLOCK0["pq"], e, query[e][:])

            def rank(it, s):
                if s % 2:
                    n, e = it * 2 + s // 2, s // 2 % 2
                    v.wait_ge(score_ready, n + 3)
                    v.wait_ge(top_kept, n + 1)
                    top, idx, sc = top_now[e], idx_now[e], score[e]
                    settle()
                    for tt in range(TT):
                        did(nc.vector.max(top[:, tt, 0:8], sc[:, tt, :]))
                    wait()
                    settle()
                    for tt in range(TT):
                        did(nc.vector.match_replace(score_b[:, tt, :], top[:, tt, 0:8], sc[:, tt, :], LOWEST))
                    for tt in range(TT):
                        did(nc.vector.max_index(idx[:, tt, 0:8], top[:, tt, 0:8], sc[:, tt, :]))
                    wait()
                    settle()
                    for tt in range(TT):
                        did(nc.vector.max(top[:, tt, 8:16], score_b[:, tt, :]))
                    wait()
                    settle()
                    nc.vector.max_index(idx[:, 0, 8:16], top[:, 0, 8:16], score_b[:, 0, :])
                    nc.vector.max_index(idx[:, 1, 8:16], top[:, 1, 8:16], score_b[:, 1, :]).then_inc(top_ready, 1)
            left = run(v, body, "pq", (keep_query, 1), (rank, 4), steps=me, per=16, carry=True)

            def keep_u(it, s):
                if s == 0:
                    sum_of(it * 2 - 1 + BLOCK0["u"], 1, upper[1][:])
                if s == 2:
                    sum_of(it * 2 + BLOCK0["u"], 0, upper[0][:])

            halves = top_s[:].rearrange("p t h c k -> p (t h) c k")
            cut, cut2 = [P, TOPK, TOPK], [P, 2, TOPK, TOPK]

            def of_head(t, it):
                return t[:].rearrange("p t (h k) -> p (t h) k", k=TOPK)[:, bass.ds(it, 1), :].rearrange("p a k -> p (a k)")

            def best(body_it, s):
                keep_u(body_it, s)
                it = body_it - 1
                if s == 0:
                    v.wait_ge(best_ready, body_it)
                    a = flat(halves[:, bass.ds(it, 1), 0, :]).unsqueeze(2).to_broadcast(cut)
                    b = flat(halves[:, bass.ds(it, 1), 1, :]).unsqueeze(1).to_broadcast(cut)
                    did(nc.vector.tensor_tensor(cand[:].rearrange("p (a b) -> p a b", a=TOPK), a, b, ALU.add))
                    wait()
                    settle()
                    did(nc.vector.max(best_s[:, 0:8], cand[:]))
                    wait()
                    settle()
                    did(nc.vector.match_replace(cand_b[:], best_s[:, 0:8], cand[:], LOWEST))
                if s == 1:
                    did(nc.vector.max_index(best_j[:, 0:8], best_s[:, 0:8], cand[:]))
                    wait()
                    settle()
                    did(nc.vector.max(best_s[:, 8:16], cand_b[:]))
                    wait()
                    settle()
                    did(nc.vector.max_index(best_j[:, 8:16], best_s[:, 8:16], cand_b[:]))
                if s == 2:
                    wait()
                    did(nc.vector.tensor_scalar(half_u[:, 0, :], best_j[:], 4, None, ALU.logical_shift_right))
                    did(nc.vector.tensor_scalar(half_u[:, 1, :], best_j[:], 15, None, ALU.bitwise_and))
                    did(nc.vector.tensor_scalar(of_head(found_g, it), best_s[:], best_s[:, 0:1], None, ALU.subtract))
                    wait()
                    did(nc.vector.tensor_copy(half_f[:], half_u[:]))
                    wait()
                    nc.vector.tensor_tensor(pick[:], half_f[:].unsqueeze(3).to_broadcast(cut2),
                                            iota16[:].unsqueeze(1).unsqueeze(1).to_broadcast(cut2), ALU.is_equal
                                            ).then_inc(picked, 1)
                if s == 3:
                    v.wait_ge(picked_row, body_it)
                    ij = found_ij[:].rearrange("p c t (h k) -> p c (t h) k", k=TOPK)[:, :, bass.ds(it, 1), :]
                    nc.vector.tensor_reduce(ij.rearrange("p c a k -> p c (a k)"), pick_b[:], AX.X, ALU.add
                                            ).then_inc(best_ready, 1)
            v.sem_inc(best_ready, 1)
            body("u", 0, lambda it, s: (carried_out(left, s), keep_u(it, s) if s else None))
            me.flat()
            v.wait_ge(iota_ready, 1)
            v.wait_ge(top_kept, HC + 2)
            with v.Fori(1, UR) as it:
                me.loop(it, 10, 1)
                body("u", it, best)
            me.end_loop(UR - 1)

            def divide(it, s):
                keep_u(it, s)
                if s == 1:
                    g = found_g[:].rearrange("p t (h k) -> p (t h) k", k=TOPK)
                    v.wait_ge(soft_ready, 1)
                    did(nc.vector.tensor_reduce(soft_sum[:], g, AX.X, ALU.add))
                    wait()
                    did(nc.vector.reciprocal(soft_sum[:], soft_sum[:]))
                    wait()
                    nc.vector.tensor_tensor(g, g, soft_sum[:].unsqueeze(2).to_broadcast([P, TT * PH, TOPK]), ALU.mult
                                            ).then_inc(found_ready, 1)
            def first_ones(it, s):
                keep_u(it, s)
                if s == 3:
                    v.wait_ge(found_turned, 3)
                    v.wait_ge(iota_ready, 2)
                    ones_of(0, 0)

            def ones_of(it, s):
                e = s % 2
                v.wait_ge(gates_spread, it * BODY + (s + 2))
                for dst, src, ready in ((one_i, ps[5], one_i_ready), (one_j[e], ps[6], one_j_ready)):
                    x = src[:, bass.ds(it * 2 * BODY + 2 * s, 2)].unsqueeze(2).to_broadcast([P, 2, P])
                    nc.vector.tensor_tensor(dst[:], x, iota128[:].unsqueeze(1).to_broadcast([P, 2, P]), ALU.is_equal
                                            ).then_inc(ready, 1)

            def gated_of(it, s):
                v.wait_ge(gates_spread, it * BODY + (s + 3))
                a2 = act[:, :, bass.ds(it * 2 * BODY + 2 * s, 2)].rearrange("p j u -> p u j")
                nc.vector.tensor_tensor(a2, a2, ps[2 + s % 2][:, 0:2 * P].rearrange("p (u j) -> p u j", u=2), ALU.mult
                                        ).then_inc(gated, 1)

            def multiplied_of(j, e):
                v.wait_ge(act_ready, j + 1)
                nc.vector.tensor_tensor(pick1(act, j), pick1(act, j), upper[e][:], ALU.mult).then_inc(multiplied, 1)

            def multiply_u(it, s):
                if s == 1:
                    multiplied_of(it * 2 - 1, 1)
                if s == 3:
                    multiplied_of(it * 2, 0)

            def spread_gates(it, s, last=False):
                g = it - U0
                if not (last and s == 3):
                    ones_of(g if s < 3 else g + 1, (s + 1) % BODY)
                keep_u(it, s)
                v.wait_ge(gated, g * BODY + (s + 2))
                if s % 2 == 0:
                    v.wait_ge(multiplied, g * 2 + (s // 2 + 2))
                gated_of(g, s)
                if s % 2:
                    v.wait_ge(gated, g * BODY + (s + 3))
                    multiply_u(it, s)

            body("u", UR, divide)
            body("u", UR + 1, first_ones)
            v.wait_ge(act_ones, TT * PH + 3)
            v.wait_ge(act_ready, J_KEPT)
            with v.Fori(U0, UG - 1) as it:
                body("u", it, spread_gates)
            body("u", UG - 1, lambda it, s: spread_gates(it, s, last=True))
            v.wait_ge(gated, PAIRS + 2)
            with v.Fori(UG, CHUNKS["u"] // BODY) as it:
                def keep_and_multiply(it, s):
                    keep_u(it, s)
                    multiply_u(it, s)
                body("u", it, keep_and_multiply)
            sum_of(NK - 1 + BLOCK0["u"], 1, upper[1][:])
            multiplied_of(NK - 1, 1)

            def act_lo_of(j, r):
                v.wait_ge(act_hi_ready, j + 1)
                nc.vector.tensor_tensor(act_lo[r][:], pick1(act, j), act_hi[r][:].bitcast(F32), ALU.subtract
                                        ).then_inc(act_lo_ready, 1)
            act_lo_of(0, 0)

            def down(it, last=False):
                for s in range(BODY):
                    if not (last and s == 3):
                        lo_of(CHUNK0["down"], it, s + 1)
                    if s % 2 == 0 and not (last and s == 2):
                        act_lo_of(it * 2 + (s // 2 + 1), (s // 2 + 1) % 2)
            with v.Fori(0, CHUNKS["down"] // BODY - 1) as it:
                down(it)
            down(CHUNKS["down"] // BODY - 1, last=True)

            v.wait_ge(x2_in, 16)
            for tt in range(TT):
                v.wait_ge(down_done, tt + 1)
                for c in range(4):
                    x = x2[:, tt, c * 512:(c + 1) * 512]
                    nc.vector.tensor_tensor(x, ps[4 * tt + c][:], x, ALU.add).then_inc(x2_ready, 1)
            v.wait_ge(g_final_in, 16)
            for tt in range(TT):
                v.wait_ge(x2_sq, tt + 1)
                m, w, r = (stat[:, 2 * n + tt:2 * n + tt + 1] for n in range(3))
                did(nc.vector.tensor_scalar(m, m, 1.0 / D, EPS, ALU.mult, ALU.add))
                wait()
                rsqrt_of(m, w, r, 3 + tt)
                for c in range(2):
                    half = slice(c * D // 2, (c + 1) * D // 2)
                    nc.vector.scalar_tensor_tensor(out=y[:, tt, half], in0=x2[:, tt, half], scalar=r, in1=g_final[:, half],
                                                   op0=ALU.mult, op1=ALU.mult).then_inc(y_ready, 1)

        @block.tensor
        def _(pe):
            def products(slot, lslot, items):
                for n, (bank, col, m, first, last) in enumerate(items):
                    def high():
                        return nc.tensor.matmul(ps[bank][:], hi[slot][:, col:col + P], m, start=first, stop=last)

                    def low():
                        return nc.tensor.matmul(ps[bank][:, 0:T], lo[lslot][:, col:col + P], m[:, 0:T], start=False,
                                                stop=False, skip_group_check=True)
                    if last:
                        low()
                        ins = high()
                    else:
                        high()
                        ins = low()
                ins.then_inc(chunk_used, 1)

            def body(name, it, src=move, after=None, before=None):
                c0, b0 = CHUNK0[name], BLOCK0[name]
                for s in range(BODY):
                    if name == "oa":
                        b = it * 4 + (b0 + s)
                        items = [(s % 2, k * P, src[:, k, :], k == 0, k == 7) for k in range(8)]
                    elif name == "ob":
                        b = it * 8 + (b0 + 2 * s)
                        items = [((s + 1) % 2 * 2 + e, (4 * e + k) * P, src[:, A_Q + k, :], k == 0, k == 3) for e in range(2) for k in range(4)]
                    else:
                        b = it * 2 + (b0 + s // 2)
                        half = s % 2
                        items = [(s // 2, k * P, src[:, 8 * half + k, :], half == 0 and k == 0, half == 1 and k == 7)
                                 for k in range(8)]
                    if before:
                        before(it, s)
                    pe.wait_ge(lo_ready, it * BODY + (c0 + s + 1))
                    if name in ("oa", "ob") or s % 2 == 0:
                        pe.wait_ge(block_summed, b if name == "ob" else b + 1)
                    products(s % RAW, s % LOS, items)
                    if after:
                        after(it, s)

            def after_body(name, it, after):
                body(name, it, after=after)

            pe.sem_inc(chunk_used, RAW)
            pe.sem_inc(vt_turned, 2)
            pe.sem_inc(scores_done, 1)
            pe.sem_inc(prob_turned, 1)
            pe.sem_inc(key_scores, 2)
            pe.sem_inc(gates_spread, 2)

            pe.wait_ge(consts, 1)
            pe.wait_ge(small_in, 16 * 3)
            nc.tensor.matmul(ps[6][0:HEADS, :], table_sb[:], rows_sb[:], start=True, stop=True).then_inc(line_sum, 1)

            def norm_there(first):
                def f(it, s):
                    if s < 2:
                        pe.wait_ge(move_ready, first + 2 * s + 2)
                return f
            def sum_squares(it, s):
                if s == 1:
                    for half in range(2):
                        pe.wait_ge(ssq_ready, half + 1)
                        ins = nc.tensor.matmul(ps[5][:, 0:T], ones[:], (ssq, ssq_b)[half][:], start=half == 0, stop=half == 1)
                    ins.then_inc(ssq_sum, 1)
            body("qk", 0, before=norm_there(0), after=sum_squares)
            with pe.Fori(1, FLIP0) as it:
                body("qk", it)

            def flip_bias(it, s):
                if s % 2 == 0:
                    h = (it - FLIP0) * 2 + s // 2
                    pe.wait_ge(bias_ready, h + 1)
                    nc.tensor.matmul(ps[6 + s // 2][:, 0:N_BIAS], flip[:], pick1(hankel, h), start=True, stop=True
                                     ).then_inc(bias_flipped, 1)
            pe.wait_ge(line_ready, 1)
            pe.wait_ge(const_in, 16 * 4)
            pe.wait_ge(bias_in, 16 * (HEADS // SLANT))
            with pe.Fori(FLIP0, CHUNKS["qk"] // BODY) as it:
                body("qk", it, after=flip_bias)

            def turn_v(it, s):
                if s % 2:
                    n, e = it * 2 + s // 2, s // 2 % 2
                    pe.wait_ge(block_summed, n + (BLOCK0["v"] + 3))
                    pe.wait_ge(vn_ready, n + 1)
                    for tt in range(TT):
                        ins = nc.tensor.transpose(ps[6 + e][:, tt * P:(tt + 1) * P], v_t[e][:, tt * P:(tt + 1) * P], ident[:])
                    ins.then_inc(vt_turned, 1)
            pe.wait_ge(bias_ready, HEADS + 2)
            left = run(pe, after_body, "v", (turn_v, 2), carry=True)

            def scores(n, q, k, banks):
                pe.wait_ge(q_staged, n + 1)
                for g in range(q):
                    for u in range(2):
                        ins = nc.tensor.matmul(ps[banks + g][:, u * T:(u + 1) * T], q_now[:, g, u * P:(u + 1) * P], k(g),
                                               start=True, stop=True)
                ins.then_inc(scores_done, 1)

            def turn_p(n, groups, bank):
                pe.wait_ge(prob_ready, n * 2 + 2)
                for g in range(groups):
                    for k in range(TT):
                        for u in range(2):
                            ins = nc.tensor.transpose(ps[bank + g][:, k * T + u * P:k * T + (u + 1) * P],
                                                      prob[:, u, g, k * P:(k + 1) * P], ident[:])
                ins.then_inc(prob_turned, 1)

            def times_v(n, copied, groups, val):
                pe.wait_ge(prob_copied, copied)
                pe.wait_ge(o_ready, n + 1)
                for g in range(groups):
                    for k in range(TT):
                        ins = nc.tensor.matmul(ps[5][:, 0:T], val(g, k), prob_t[:, g, k, :], start=g == 0 and k == 0,
                                               stop=g == groups - 1 and k == TT - 1)
                ins.then_inc(pv_done, 1)

            def head(h, kv, carried=()):
                def heads_a(it, s):
                    carried_out(carried, s)
                    if s == 1:
                        turn_p(h, 1, 3)
                scores(h, 1, lambda g: qk[:, A_Q + B_H + kv, :], 2)
                body("gate", h, after=heads_a)
                if carried:
                    pe.wait_ge(vn_ready, N_V + 2)
                times_v(h, h + 1, 1, lambda g, k: v_nat[:, k, kv, :])
            head(0, 0, carried=left)
            for kv in range(A_KV):
                with pe.Fori(max(1, kv * A_GROUP), (kv + 1) * A_GROUP) as h:
                    head(h, kv)
            with pe.Fori(0, B_S) as s4:
                def heads_b(it, s):
                    if s == 1:
                        turn_p(s4 + A_Q, B_G, 2)
                scores(s4 + A_Q, B_G, lambda g: pick1(qk, s4 + (A_Q + B_H + A_KV + g * B_S)), 2)
                body("gate", s4 * 2 + A_Q)
                body("gate", s4 * 2 + (A_Q + 1), after=heads_b)
                pe.wait_ge(v_staged, s4 * 2 + 2)
                times_v(s4 + A_Q, s4 * B_G + (A_Q + B_G), B_G, lambda g, k: v_now[:, k, g, :])

            pe.wait_ge(att_ready, 3)
            with pe.Fori(0, CHUNKS["oa"] // BODY) as it:
                body("oa", it, att)
            pe.wait_ge(att_ready, 4)
            with pe.Fori(0, CHUNKS["ob"] // BODY) as it:
                body("ob", it, att)
            def merged_there(it, s):
                if s < 2:
                    pe.wait_ge(merged_lo, (s + 1) * KT // 2 + 4)
            body("out", 0, before=merged_there)
            with pe.Fori(1, CHUNKS["out"] // BODY) as it:
                body("out", it)

            pe.wait_ge(sq_added, KT + 2)
            nc.tensor.matmul(ps[5][:, 0:T], ones[:], ssq[:], start=True, stop=True).then_inc(ssq_sum, 1)
            for n in range(8):
                if n >= TURNS:
                    pe.wait_ge(x1_copied, n - TURNS + 1)
                for k in range(4):
                    ins = nc.tensor.transpose(ps[TURN_BANKS[n % TURNS]][:, k * P:(k + 1) * P],
                                              x1[:, n % 4 * 4 + k, n // 4 * P:(n // 4 + 1) * P], ident[:])
                ins.then_inc(x1_turned, 1)

            def score_keys(it, s):
                if s % 2:
                    n, e = it * 2 + s // 2, s // 2 % 2
                    pe.wait_ge(block_summed, n + (BLOCK0["pq"] + 3))
                    pe.wait_ge(score_ready, n + 1)
                    for tt in range(TT):
                        ins = nc.tensor.matmul(ps[6 + e][:, tt * NK:(tt + 1) * NK], query[e][:, tt * P:(tt + 1) * P],
                                               pick1(keys_sb, n), start=True, stop=True)
                    ins.then_inc(key_scores, 1)
            def pq_there(it, s):
                norm_there(4)(it, s)
                if s == 2:
                    pe.wait_ge(keys_in, 16)
                    pe.wait_ge(x1_copied, 8)

            def pq_body(name, it, after):
                body(name, it, after=after, before=pq_there if isinstance(it, int) else None)
            left = run(pe, pq_body, "pq", (score_keys, 2), carry=True)

            body("u", 0, after=lambda it, s: carried_out(left, s))
            with pe.Fori(1, UR + 1) as it:
                body("u", it)
            pe.wait_ge(found_ready, 1)
            for n, t in enumerate((found_g[:], found_ij[:, 0, :, :], found_ij[:, 1, :, :])):
                for tt in range(TT):
                    ins = nc.tensor.transpose(ps[4 + n][:, tt * P:(tt + 1) * P], t[:, tt, :], ident[:])
                ins.then_inc(found_turned, 1)

            body("u", UR + 1)
            def spread_gates(it, s):
                n = (it - U0) * BODY
                pe.wait_ge(one_i_ready, n + (s + 1))
                pe.wait_ge(one_j_gated, n + (s + 1))
                pe.wait_ge(gated, n + (s + 1))
                for u in range(2):
                    ins = nc.tensor.matmul(ps[2 + s % 2][:, u * P:(u + 1) * P], one_i[:, u, :], one_j[s % 2][:, u, :],
                                           start=True, stop=True)
                ins.then_inc(gates_spread, 1)
            with pe.Fori(U0, UG) as it:
                body("u", it, before=spread_gates)
            with pe.Fori(UG, CHUNKS["u"] // BODY) as it:
                body("u", it)
            pe.drain().then_inc(move_free, 1)

            pe.wait_ge(zero_ready, 1)
            pe.wait_ge(gated, PAIRS + 2)
            for b in (2, 3, 4, 5, 6, 7, 0, 1):
                if b == 0:
                    pe.wait_ge(block_summed, BLOCK0["u"] + BLOCKS["u"] + 2)
                nc.tensor.matmul(ps[b][:], zero[:, 0:P], zero[:], start=True, stop=False)

            def down(s, tt, last=False):
                r = s // 2
                for n, (a, w) in enumerate(((act_hi[r], hi[s]), (act_hi[r], lo[s % LOS]), (act_lo[r], hi[s]))):
                    for c in range(2):
                        stop = last and n == 2
                        ins = nc.tensor.matmul(ps[4 * tt + 2 * (s % 2) + c][:], a[:, tt * P:(tt + 1) * P],
                                               w[:, c * 512:(c + 1) * 512], start=False, stop=stop,
                                               skip_group_check=not stop)
                return ins

            def down_there(it, s):
                pe.wait_ge(lo_ready, it * BODY + (CHUNK0["down"] + s + 1))
                if s % 2 == 0:
                    pe.wait_ge(act_lo_ready, it * 2 + (s // 2 + 1))

            def down_body(it, steps):
                for s in steps:
                    down_there(it, s)
                    for tt in range(TT):
                        ins = down(s, tt)
                    ins.then_inc(chunk_used, 1)
            last = CHUNKS["down"] // BODY - 1
            with pe.Fori(0, last) as it:
                down_body(it, range(BODY))
            down_body(last, range(2))
            down_there(last, 2)
            down_there(last, 3)
            for tt in range(TT):
                down(2, tt, last=True)
                down(3, tt, last=True).then_inc(down_done, 1)


def spread(ap, n):
    return bass.AP(ap.tensor, 0, [[0, P], [1, n]])


def slant(line, h, n):
    return bass.AP(line, h * N_DELTA, [[1, P], [N_DELTA, n], [1, N_BIAS]])


def columns(w, order=None):
    k, n = w.shape
    b = w.reshape(k // P, P, n // P, P).transpose(2, 1, 0, 3)
    if order is not None:
        b = b[order]
    b = b.reshape(b.shape[0], P, k)
    if k > CW:
        b = b.reshape(b.shape[0], P, k // CW, CW).transpose(0, 2, 1, 3)
    elif k < CW:
        b = b.reshape(b.shape[0] * k // CW, CW // k, P, k).transpose(0, 2, 1, 3)
    return np.ascontiguousarray(b.reshape(-1, P, CW))


def kernel(**inputs):
    import concourse.bacc as bacc
    from concourse.bass_utils import run_bass_kernel_spmd

    f = {k: np.asarray(v) for k, v in inputs.items()}
    aq, akv, b = A_Q, A_KV, B_H
    w_in = f["w_in"][0]
    order = np.arange(w_in.shape[1] // P)
    qa, ka, va, qb, kb, vb, rest = np.split(order, np.cumsum([aq, akv, akv, b, b, b]))
    x_t = np.ascontiguousarray(f["x"][0].reshape(T, KT, P).transpose(2, 1, 0))
    arrays = {
        "x_t": x_t,
        "g_mix": np.ascontiguousarray(f["norm_mix_g"][0].reshape(KT, P).T),
        "g_ffn": np.ascontiguousarray(f["norm_ffn_g"][0].reshape(KT, P).T),
        "g_final": f["norm_final_g"],
        "ident": np.eye(P, dtype=np.float32),
        "flip": np.ascontiguousarray(np.eye(P, dtype=np.float32)[::-1]),
        "bias_rows": bias_rows(),
        "head_kinds": head_kinds(),
        "rel_bias": f["rel_bias"],
        "sink_a": f["sink_a"][0],
        "keys": np.ascontiguousarray(f["peer_keys"][0].reshape(HC, NK, HD).transpose(2, 0, 1)),
        "w_qk": columns(w_in, np.concatenate([qa, qb, ka, kb])),
        "w_v": columns(w_in, np.concatenate([va, vb])),
        "w_gate": columns(w_in, rest),
        "w_oa": columns(f["w_oa"][0]),
        "w_ob": columns(f["w_ob"][0]),
        "w_out": columns(f["w_out"][0]),
        "w_pq": columns(f["peer_wq"][0]),
        "w_u": np.ascontiguousarray(f["peer_u"][0].reshape(NK, NK, 2, 8, P).transpose(1, 2, 4, 3, 0).reshape(-1, P, CW)),
        "w_down": np.ascontiguousarray(f["peer_v"][0].reshape(NK, NK, 2, CW).transpose(1, 2, 0, 3).reshape(-1, P, CW)),
    }
    nc = bacc.Bacc("TRN2", target_bir_lowering=False, num_devices=1)
    aps = {k: nc.dram_tensor(k, a.shape, F32, kind="ExternalInput").ap() for k, a in arrays.items()}
    out = nc.dram_tensor("out", [T, D], F32, kind="ExternalOutput").ap()
    build(nc, aps, out)
    r = run_bass_kernel_spmd(nc, [arrays], core_ids=[0])
    return r.results[0]["out"].reshape(1, T, D)
```
